# Optimizing a Trainium2 kernel written in Bass

```python
import jax, jax.numpy as jnp
from jax import lax
import numpy as np

D_MODEL = 1024
BATCH = 1
SEQ = 1024
DEPTH = 1

HGRN_HEADS = 4
HGRN_DK = 128
HGRN_DV = 128
HGRN_WIDTH = HGRN_HEADS * HGRN_DK
CHUNK = 64
ATTN_HEADS = 8
ATTN_KV_HEADS = 2
ATTN_GROUP = ATTN_HEADS // ATTN_KV_HEADS
ATTN_HD = 64
ATTN_WIDTH = ATTN_HEADS * ATTN_HD
KV_WIDTH = ATTN_KV_HEADS * ATTN_HD
WINDOW = 128
BLOCK = 128
MIX_WIDTH = HGRN_HEADS * HGRN_DV + ATTN_WIDTH
PROJ_WIDTH = 4 * HGRN_WIDTH + ATTN_WIDTH + 2 * KV_WIDTH
SPLITS = [HGRN_WIDTH, 2 * HGRN_WIDTH, 3 * HGRN_WIDTH, 4 * HGRN_WIDTH,
          4 * HGRN_WIDTH + ATTN_WIDTH, 4 * HGRN_WIDTH + ATTN_WIDTH + KV_WIDTH]
D_FF = -(-8 * D_MODEL // (3 * 256)) * 256
EPS = 1e-6
NEG_INF = -1e30

kernel_name = "hymba_hgrn2_swa_sink_block"

def rms_norm(x, gain):
    xf = x.astype(jnp.float32)
    y = xf * lax.rsqrt(jnp.mean(xf * xf, axis=-1, keepdims=True) + EPS)
    return (y * gain.astype(jnp.float32)).astype(x.dtype)

def hgrn2_mixer(q, f_logit, i, g, lb, out_gain):
    B, S, _ = q.shape
    f32 = jnp.float32
    lb = lb.astype(f32)
    q = jax.nn.silu(q.astype(f32)) * (HGRN_DK ** -0.5)
    f = lb + (1.0 - lb) * jax.nn.sigmoid(f_logit.astype(f32))
    k = 1.0 - f
    logf = jnp.log(f)
    v = i.astype(f32)
    nc = S // CHUNK

    def to_chunks(t, d):
        return t.reshape(B, nc, CHUNK, HGRN_HEADS, d).transpose(1, 0, 3, 2, 4)

    xs = (to_chunks(q, HGRN_DK), to_chunks(k, HGRN_DK), to_chunks(v, HGRN_DV), to_chunks(logf, HGRN_DK))
    causal = jnp.tril(jnp.ones((CHUNK, CHUNK), dtype=bool))[:, :, None]

    def step(state, inp):
        qb, kb, vb, gb = inp
        bcum = jnp.cumsum(gb, axis=2)
        diff = bcum[:, :, :, None, :] - bcum[:, :, None, :, :]
        decay = jnp.exp(jnp.where(causal, diff, NEG_INF))
        scores = jnp.einsum('bhtc,bhsc,bhtsc->bhts', qb, kb, decay)
        o_intra = jnp.einsum('bhts,bhsv->bhtv', scores, vb)
        o_inter = jnp.einsum('bhtc,bhcv->bhtv', qb * jnp.exp(bcum), state)
        btot = bcum[:, :, -1:, :]
        k_dec = kb * jnp.exp(btot - bcum)
        new_state = jnp.exp(btot[:, :, 0, :])[..., None] * state + jnp.einsum('bhsc,bhsv->bhcv', k_dec, vb)
        return new_state, o_intra + o_inter

    s0 = jnp.zeros((B, HGRN_HEADS, HGRN_DK, HGRN_DV), f32)
    _, o = lax.scan(step, s0, xs)
    o = o.transpose(1, 0, 3, 2, 4).reshape(B, S, HGRN_HEADS, HGRN_DV)
    o = rms_norm(o, out_gain).reshape(B, S, HGRN_HEADS * HGRN_DV)
    return o * jax.nn.silu(g.astype(f32))

def swa_sink_mixer(q, k, v, q_gain, k_gain, sinks):
    B, S, _ = q.shape
    f32 = jnp.float32
    q = rms_norm(q.astype(f32).reshape(B, S, ATTN_KV_HEADS, ATTN_GROUP, ATTN_HD), q_gain) * (ATTN_HD ** -0.5)
    k = rms_norm(k.astype(f32).reshape(B, S, ATTN_KV_HEADS, ATTN_HD), k_gain)
    v = v.astype(f32).reshape(B, S, ATTN_KV_HEADS, ATTN_HD)
    nb = S // BLOCK

    def band(t):
        prev = jnp.pad(t, ((0, 0), (BLOCK, 0), (0, 0), (0, 0)))[:, :S]
        cur_b = t.reshape(B, nb, BLOCK, ATTN_KV_HEADS, ATTN_HD)
        prev_b = prev.reshape(B, nb, BLOCK, ATTN_KV_HEADS, ATTN_HD)
        return jnp.concatenate([prev_b, cur_b], axis=2)

    kb, vb = band(k), band(v)
    qb = q.reshape(B, nb, BLOCK, ATTN_KV_HEADS, ATTN_GROUP, ATTN_HD)
    scores = jnp.einsum('bnqhgd,bnkhd->bnhgqk', qb, kb)
    n_idx = jnp.arange(nb)[:, None, None]
    qpos = n_idx * BLOCK + jnp.arange(BLOCK)[None, :, None]
    kpos = n_idx * BLOCK - BLOCK + jnp.arange(2 * BLOCK)[None, None, :]
    rel = qpos - kpos
    mask = (rel >= 0) & (rel < WINDOW) & (kpos >= 0)
    scores = jnp.where(mask[None, :, None, None], scores, NEG_INF)
    s = sinks.astype(f32).reshape(ATTN_KV_HEADS, ATTN_GROUP)[None, None, :, :, None, None]
    m = jnp.maximum(jnp.max(scores, axis=-1, keepdims=True), s)
    p = jnp.exp(scores - m)
    denom = jnp.sum(p, axis=-1, keepdims=True) + jnp.exp(s - m)
    out = jnp.einsum('bnhgqk,bnkhd->bnqhgd', p / denom, vb)
    return out.reshape(B, S, ATTN_WIDTH)

def setup_inputs(seed: int = 0) -> dict:
    key = jax.random.key(seed)
    ks = jax.random.split(key, 14)
    f32 = jnp.float32
    nrm = lambda k, shape, scale: jax.random.normal(k, shape, f32) * scale
    return {
        "x": jax.random.normal(ks[0], (BATCH, SEQ, D_MODEL), f32),
        "norm1_gain": 1.0 + nrm(ks[1], (DEPTH, D_MODEL), 0.02),
        "w_in": nrm(ks[2], (DEPTH, D_MODEL, PROJ_WIDTH), D_MODEL ** -0.5),
        "hgrn_lb_logits": nrm(ks[3], (DEPTH + 1, HGRN_WIDTH), 0.5),
        "hgrn_out_gain": 1.0 + nrm(ks[4], (DEPTH, HGRN_DV), 0.02),
        "q_norm_gain": 1.0 + nrm(ks[5], (DEPTH, ATTN_HD), 0.02),
        "k_norm_gain": 1.0 + nrm(ks[6], (DEPTH, ATTN_HD), 0.02),
        "attn_sinks": nrm(ks[7], (DEPTH, ATTN_HEADS), 0.5),
        "w_out": nrm(ks[8], (DEPTH, MIX_WIDTH, D_MODEL), MIX_WIDTH ** -0.5),
        "norm2_gain": 1.0 + nrm(ks[9], (DEPTH, D_MODEL), 0.02),
        "w_ffn_gate": nrm(ks[10], (DEPTH, D_MODEL, D_FF), D_MODEL ** -0.5),
        "w_ffn_up": nrm(ks[11], (DEPTH, D_MODEL, D_FF), D_MODEL ** -0.5),
        "w_ffn_down": nrm(ks[12], (DEPTH, D_FF, D_MODEL), D_FF ** -0.5),
    }

def reference(x, norm1_gain, w_in, hgrn_lb_logits, hgrn_out_gain, q_norm_gain, k_norm_gain,
              attn_sinks, w_out, norm2_gain, w_ffn_gate, w_ffn_up, w_ffn_down):
    h = x
    lb_all = jnp.cumsum(jax.nn.softmax(hgrn_lb_logits.astype(jnp.float32), axis=0), axis=0)
    for l in range(DEPTH):
        u = rms_norm(h, norm1_gain[l])
        proj = u @ w_in[l]
        hq, hf, hi, hg, aq, ak, av = jnp.split(proj, SPLITS, axis=-1)
        o_rec = hgrn2_mixer(hq, hf, hi, hg, lb_all[l], hgrn_out_gain[l])
        o_att = swa_sink_mixer(aq, ak, av, q_norm_gain[l], k_norm_gain[l], attn_sinks[l])
        mixed = jnp.concatenate([o_rec, o_att], axis=-1).astype(h.dtype)
        h = h + mixed @ w_out[l]
        u = rms_norm(h, norm2_gain[l])
        h = h + (jax.nn.silu(u @ w_ffn_gate[l]) * (u @ w_ffn_up[l])) @ w_ffn_down[l]
    return h


_drawn_inputs = setup_inputs


def setup_inputs(seed=0):
    import zlib

    import numpy as np

    out = dict(_drawn_inputs(seed))
    spreads = {}
    factors = {'norm1_gain': 4.031,
     'hgrn_out_gain': 6.507,
     'q_norm_gain': 8.0,
     'k_norm_gain': 8.0,
     'attn_sinks': 64.0,
     'norm2_gain': 12.306}
    for name, (base, spread) in spreads.items():
        noise = np.random.default_rng([zlib.crc32(name.encode()), seed]).standard_normal(out[name].shape)
        drawn = base * np.exp(spread * noise) if base else spread * noise
        out[name] = __import__('jax').numpy.asarray(drawn.astype(out[name].dtype))
    for name, factor in factors.items():
        out[name] = (out[name] * factor).astype(out[name].dtype)
    return out
```

```python
from contextlib import ExitStack

import concourse.bass as bass
from concourse import mybir

ALU = mybir.AluOpType
ACT = mybir.ActivationFunctionType
AX = mybir.AxisListType
F32 = mybir.dt.float32
F32R = mybir.dt.float32r
BF16 = mybir.dt.bfloat16
I8 = mybir.dt.int8

P = 128
D = 1024
T = 1024
KT = D // P
HALF = 512
NH = 4
NC = T // P
HD = 64
AH, KVH = 8, 2
GRP = AH // KVH
VW = (NH * P + KVH * HD) // 2
F = 2816
FT = F // P
EPS = 1e-6
TINY = 1e-18
NEG = -1e30
LEVELS = 7
KB = 1024
N_PROJ = 5 + 3 * NH
N_UNITS = N_PROJ + 9
V_FIRST = 6
LAG = 3


def schedule():

    def proj(tiles):
        return [("P", 2 * u + half, part) for u in tiles for half in range(2) for part in range(4)]

    def tile(hd, j):
        return 5 + 3 * hd + j

    def out(group):
        parts = (2, 2, 1)[group]
        return [("O", 16 * group + g, part) for g in range(16) for part in range(parts)]

    def weights_after(d):
        if d[0] == "P" and d[1] % 2 == 1 and d[2] == 3:
            return d[1] // 2 + 2
        if d[0] == "O" and d[1] < 32 and d[1] % 4 == 3 and d[2] == 1:
            return N_PROJ + d[1] // 4 + 2
        return N_UNITS

    def mix(dense, steps, lead=0):
        res, k, n = [], 0, len(dense) - lead
        for seen, d in enumerate(dense, 1):
            res.append(d)
            if weights_after(d) < N_UNITS:
                res.append(("W", weights_after(d)))
            while k < len(steps) and seen >= lead and k * n <= (seen - lead) * len(steps):
                res += steps[k]
                k += 1
        for s in steps[k:]:
            res += s
        return res

    order = [("W", 0), ("W", 1)]
    order += [("V", n, t) for n in range(2) for t in range(NC) if (n, t) >= (0, V_FIRST)]
    for u in range(5):
        order += mix(proj([u]), [[("AM", u - 1)], [("AN", u - 1)]] if u else [], lead=3)
        order += [("AS", u)]
    f0 = proj([tile(0, 0)])
    order += mix(f0[:4], [[("AM", 4)], [("AN", 4)]], lead=2)
    units = 2 * NC
    steps = []
    for i in range(units + LAG + 1):
        steps.append([s for s in (("PV", i - LAG - 1), ("TR", i - LAG), ("SC", i), ("SN", i - 1))
                      if 0 <= s[1] < units])
    order += mix(f0[4:] + proj([tile(0, 1), tile(0, 2)]), steps, lead=1)
    order += [("H1", 0)]
    order += mix(proj([tile(1, 0)]), [[("H2", 0)], [("KT", 0), ("KE", 0), ("LV", 0, 0)], [("LV", 0, 1)]], lead=2)
    for h in range(NH):
        last = h == NH - 1
        steps = []
        for lv in range(LEVELS + 1):
            steps.append([("LM", h, lv)] + ([("LV", h, lv + 2)] if lv + 2 < LEVELS else []))
        if h:
            steps[1] += [("OM", h - 1)]
            steps[2] += [("ON", h - 1)]
            if last:
                steps[3] += [("FD", 1), ("FD", 0), ("MS", 6)]
        if not last:
            order += mix(proj([tile(h + 1, 1), tile(h + 1, 2)]), steps)
            if h == NH - 2:
                order += [("MS", i) for i in range(4)]
            order += [("H1", h + 1)]
        else:
            order += mix(out_a[8:], steps)
            order += [("FD", 2), ("FD", 3), ("F", 0)]
        steps = [[("OC", h, c)] for c in range(NC)]
        if not last:
            steps[1] += [("H2", h + 1)]
            steps[2] += [("LV", h + 1, 0)]
            steps[4] += [("KT", h + 1)]
            steps += [[("OS", h), ("KE", h + 1), ("LV", h + 1, 1)]]
        else:
            steps += [[("OS", h)], [("OM", h)], [("ON", h)], [("MS", 7)]]
            steps[2] += [("F", 1)]
            steps[5] += [("F", 2)]
        if h < NH - 2:
            order += mix(proj([tile(h + 2, 0)]), steps)
        elif h == NH - 2:
            order += [("MS", 4), ("MS", 5)] + steps[0] + steps[1]
            out_a = out(0)
            order += mix(out_a[:8], steps[2:])
        else:
            order += mix(out(1), steps)
    order += [("FD", 4), ("FD", 5)] + [("O", 32 + g, 0) for g in range(2)]
    for m in range(KT):
        order += [("O", 34 + 2 * m + half, 0) for half in range(2) if m < KT - 1]
        order += [("N2", m)]
    order += [("F", 3), ("F", 4), ("F", 5)]
    return order


def build(nc, xT, wv, wproj, wo_a, wo_b, wo_c, wg, wu, wd, gain1, gain2, lbl, ogain, qgain, kgain, sinks, yT):
    ctx = ExitStack()
    with ctx:
        used = {}

        def at(name, kb, shape, dt=F32):
            return nc.alloc_sbuf_tensor_at(name, shape, dt, offset=16640 + int(kb * KB))

        def sem(name):
            return ctx.enter_context(nc.semaphore(name))

        ones = at("ones", 0, [P, P])
        ident = at("ident", 0.5, [P, P])
        blk = at("blk", 1, [P, P])
        wmask = at("wmask", 1.5, [P, 2 * P])
        lmask = at("lmask", 2.5, [P, LEVELS + 1, P], I8)
        scan_keep = at("scan_keep", 3.5, [P, T], BF16)
        S = at("S", 5.5, [P, 2, P])
        small = at("small", 6.5, [P, 120])
        g1, g2 = small[:, 0:8], small[:, 8:16]
        lb_in = small[:, 16:24]
        lb_e, lb_m = small[:, 24:32], small[:, 32:36]
        lb, omlb, nomlb = small[:, 36:40], small[:, 40:44], small[:, 44:48]
        og, qg, kg = small[:, 48:49], small[:, 49:50], small[:, 50:51]
        eps = small[:, 51:52]
        sink, nsink = small[:, 52:60], small[:, 60:68]
        ebt = small[:, 68:84]
        lb_s = small[:, 84:88]
        rtok = small[:, 88:96]
        smax = at("smax", 207, [P, 60])
        nmax, rsum, esink, den, rden = (smax[:, 12 * i:12 * i + 12] for i in range(5))
        uhi = at("uhi", 7, [P, KT, T], F32R)
        ulo = at("ulo", 39, [P, KT, T], F32R)
        h = at("h", 7, [P, KT, T])
        mhi0 = at("mhi0", 39, [P, 4, T], F32R)
        mlo0 = at("mlo0", 55, [P, 4, T], F32R)
        v = at("v", 71, [P, NC, 2 * VW])
        sq = at("sq", 71, [P, 4, T])
        mhi3 = at("mhi3", 71, [P, T], F32R)
        mlo3 = at("mlo3", 75, [P, T], F32R)
        x = at("x", 91, [P, KT, T])
        att = at("att", 91, [P, 4, T])
        rec = at("rec", 107, [P, NH, T])
        mhi1 = at("mhi1", 91, [P, 4, T], F32R)
        mlo1 = at("mlo1", 107, [P, NH, T], F32R)
        wraw = [at(f"wraw{i}", 123 + 4 * i, [P, KT * P]) for i in range(2)]
        whi = [at(f"whi{i}", 131 + 4 * i, [P, KT * P], F32R) for i in range(2)]
        wlo = [at(f"wlo{i}", 139 + 4 * i, [P, KT * P], F32R) for i in range(2)]
        vraw = at("vraw", 147, [P, KT * VW])
        vhi = [at(f"vhi{i}", 157 + 10 * i, [P, KT * VW], F32R) for i in range(2)]
        vlo = [at(f"vlo{i}", 177 + 10 * i, [P, KT * VW], F32R) for i in range(2)]
        kq = at("kq", 147, [P, 5, T])
        sc = at("sc", 167, [P, 3, GRP, 2 * P])
        asq = at("asq", 167, [P, 2, T])
        pT = at("pT", 179, [P, 2, GRP * P])
        ars = at("ars", 183, [P, T])
        K = at("K", 147, [P, T])
        Q = at("Q", 151, [P, T])
        B = at("B", 155, [P, T])
        DD = [at("D0", 159, [P, T]), at("D1", 163, [P, T])]
        M = [at("M0", 167, [P, T]), at("M1", 171, [P, T])]
        A = at("A", 175, [P, T])
        X0 = at("X0", 179, [P, T])
        KDT = at("KDT", 183, [P, NC, P])
        rawf, rawq = at("rawf", 187, [P, T]), at("rawq", 191, [P, T])
        rawg = [at("rawg0", 195, [P, T]), at("rawg1", 199, [P, T])]
        rs = at("rs", 203, [P, T])

        def qi(hh):
            return rec[:, hh + 1, :] if hh < NH - 1 else X0[:, :]

        def on_tmp(hh):
            return (X0, X0, rawf, M[0])[hh]

        u2hi = at("u2hi", 39, [P, KT, T], F32R)
        u2lo = at("u2lo", 91, [P, KT, T], F32R)
        nsq = at("nsq", 79, [P, 2, T])
        nrs = at("nrs", 131, [P, T])
        hidhi = at("hidhi", 71, [P, 2, T], F32R)
        hidlo = at("hidlo", 79, [P, 2, T], F32R)
        gate = [at("gate01", 87, [P, 2, HALF]), at("gate23", 123, [P, 2, HALF])]
        hid = at("hid", 127, [P, 2, HALF])
        fraw = [at(f"fraw{p}", kb, [P, KT * P]) for p, kb in enumerate((187, 191, 155, 171, 179, 167))]
        fhi = [at(f"fhi{p}", kb, [P, KT * P], F32R) for p, kb in enumerate((195, 147, 159, 175, 199, 139))]
        flo = [at(f"flo{p}", kb, [P, KT * P], F32R) for p, kb in enumerate((203, 151, 163, 183, 135, 143))]

        ps = ctx.enter_context(nc.psum_tensor("ps", [P, 8, HALF], F32))

        s_const, s_g1 = sem("consts_in"), sem("gain1_in")
        s_x = [sem(f"x_in{k}") for k in range(KT)]
        s_vraw = [sem(f"vraw_in{i}") for i in range(2)]
        s_vhi, s_vlo = sem("v_weights_hi"), sem("v_weights_lo")
        s_wraw = [sem("wraw0_in"), sem("wraw1_in")]
        s_whi, s_wlo = sem("unit_hi"), sem("unit_lo")
        s_pool0, s_setup = sem("pool_setup_step"), sem("setup_done")
        s_lb = sem("lb_step")
        s_lbact = sem("lb_exp")
        s_sq, s_ss, s_ln, s_rs = sem("n1_square"), sem("n1_sum"), sem("n1_ln"), sem("n1_rstd")
        s_uhi, s_ulo = sem("u_hi"), sem("u_lo")
        s_rt, s_rtok = sem("rstd_t"), sem("rstd_by_token")
        s_vmm, s_vev = sem("value_group"), sem("value_evac")
        s_pmm, s_pev = sem("proj_group"), sem("proj_evac")
        s_asq, s_ass, s_aln, s_ars, s_an = sem("an_sq"), sem("an_sum"), sem("an_ln"), sem("an_rstd"), sem("an_done")
        s_scm, s_masked, s_amx, s_anm, s_asn = (sem("scores"), sem("scores_masked"), sem("row_max"),
                                                sem("row_nmax"), sem("sink_arg"))
        s_exp, s_den, s_rden, s_prob = sem("att_exp"), sem("att_den"), sem("att_rden"), sem("probs")
        s_tr, s_pte0, s_pte1 = sem("probs_t"), sem("probs_t_prev_evac"), sem("probs_t_cur_evac")
        s_pv, s_attev = sem("att_out"), sem("att_out_evac")
        s_sig, s_kq, s_lnf, s_scan, s_gm = sem("sigmoids"), sem("k_and_q"), sem("log_f"), sem("decay_sums"), sem("swish_g")
        s_eb, s_qi, s_d2, s_e2, s_kd = sem("exp_b"), sem("qi"), sem("tail_sum"), sem("exp_tail"), sem("kd")
        s_kt, s_kte = sem("kd_t"), sem("kd_t_evac")
        s_lvs, s_lve, s_lvm, s_lmm, s_cp = sem("lv_sub"), sem("lv_exp"), sem("lv_mul"), sem("lv_product"), sem("lv_kept")
        s_oc, s_st, s_oev = sem("chunk_products"), sem("state"), sem("o_evac")
        s_osq, s_oss, s_oln, s_ors, s_on1, s_on = (sem("o_square"), sem("o_sum"), sem("o_ln"), sem("o_rstd"),
                                                   sem("o_normed"), sem("o_done"))
        s_mhi, s_mlo = sem("mix_hi"), sem("mix_lo")
        s_omm, s_oadd = sem("out_group"), sem("out_added")
        s_nsq, s_nss, s_nln, s_nrs = sem("n2_square"), sem("n2_sum"), sem("n2_ln"), sem("n2_rstd")
        s_u2hi, s_u2lo = sem("u2_hi"), sem("u2_lo")
        s_fraw = [sem(f"fraw{p}_in") for p in range(6)]
        s_fhi, s_flo = sem("ffn_w_hi"), sem("ffn_w_lo")
        s_gsc, s_gr = sem("gate_scaled"), sem("silu_scaled")
        s_fmm, s_silu, s_hid, s_hhi, s_hlo = (sem("gate_up_group"), sem("gate_silu"), sem("hidden"),
                                              sem("hidden_hi"), sem("hidden_lo"))
        s_dmm, s_dadd = sem("down_group"), sem("down_added")
        s_out = sem("y_out")

        order = schedule()
        N_CONST = 6
        VP = KT * VW // 2

        def nk(i):
            return P if i < 2 else 2 * P

        def tr_count(i):
            return i + 1 if i < 2 else 2 * i

        def unit_used(u):
            return (s_pmm, 2 * (u + 1)) if u < N_PROJ else (s_omm, 4 * (u - N_PROJ + 1))

        def out_bank(g):
            return (2 * N_PROJ + g) % 3 if g < 32 else g % 2

        def ffn_bank(first, p, half):
            return ((3, 4), (5, 6), (0, 1), (2, 7))[p][half] if first else 2 * p + half

        block = ctx.enter_context(nc.Block())

        @block.sync
        def _(sp):
            xv = xT.rearrange("(k p) t -> k p t", p=P)
            sp.dma_start(g1, gain1).then_inc(s_g1, 16)
            for k in range(KT):
                sp.dma_start(x[:, k, :], xv[k, :, :]).then_inc(s_x[k], 16)
                if k < 2:
                    sp.dma_start(vraw[:, k * VP:(k + 1) * VP], wv[0, :, k * VP:(k + 1) * VP]).then_inc(s_vraw[k], 16)
            for dst, src in ((g2, gain2), (lb_in, lbl), (og, ogain), (sink, sinks), (qg, qgain), (kg, kgain)):
                sp.dma_start(dst, src).then_inc(s_const, 16)
            for step in order:
                if step[0] == "W":
                    u = step[1]
                    if u >= 2:
                        sp.wait_ge(s_wlo, u - 1)
                    if u < N_PROJ:
                        src = wproj[u, :, :]
                    elif u < N_PROJ + 4:
                        src = wo_a[u - N_PROJ, :, :]
                    elif u < N_PROJ + 8:
                        src = wo_b[u - N_PROJ - 4, :, :]
                    else:
                        src = wo_c
                    sp.dma_start(wraw[u % 2][:, 0:src.shape[1]], src).then_inc(s_wraw[u % 2], 16)
                if step == ("W", 1):
                    for i in range(2):
                        sp.wait_ge(s_vlo, i + 1)
                        sp.dma_start(vraw[:, i * VP:(i + 1) * VP], wv[1, :, i * VP:(i + 1) * VP])\
                            .then_inc(s_vraw[i], 16)
                if step == ("MS", 0):
                    sp.wait_ge(s_pmm, 2 * N_PROJ)
                    for k in range(KT):
                        sp.dma_start(h[:, k, :], xv[k, :, :]).then_inc(s_x[k], 16)
                if step[0] == "FD":
                    p = step[1]
                    sp.wait_ge(*((s_on, 3), (s_kq, 8), (s_lmm, 64), (s_lmm, 64), (s_oc, 32), (s_on, 4))[p])
                    sp.dma_start(fraw[p][:, :], (wg[0], wu[0], wg[1], wu[1], wd[0], wd[1])[p]).then_inc(s_fraw[p], 16)
            with sp.Fori(0, FT // 2 - 1) as i:
                for p in range(6):
                    sp.wait_ge(s_flo, 6 * i + (p + 1))
                    w = (wg, wu, wg, wu, wd, wd)[p]
                    j = (0, 0, 1, 1, 0, 1)[p]
                    sp.dma_start(fraw[p][:, :], w[bass.ds(2 * i + (2 + j), 1), :, :].rearrange("a p n -> (a p) n"))\
                        .then_inc(s_fraw[p], 16)
            yv = yT.rearrange("(k p) t -> k p t", p=P)
            for m in range(KT):
                sp.wait_ge(s_dadd, 16 * (FT // 2 - 1) + 2 * m + 2)
                sp.dma_start(yv[m, :, :], h[:, m, :]).then_inc(s_out, 16)
            sp.wait_ge(s_out, 16 * KT)

        @block.gpsimd
        def _(pool):
            n0 = [0]

            def step0(ins):
                n0[0] += 1
                ins.then_inc(s_pool0, 1)
                pool.wait_ge(s_pool0, n0[0])

            step0(nc.gpsimd.memset(ones[:, :], 1.0))
            step0(nc.gpsimd.memset(eps, EPS))
            step0(nc.gpsimd.memset(ident[:, :], 0.0))
            step0(nc.gpsimd.affine_select(out=ident[:, :], in_=ident[:, :], compare_op=ALU.not_equal, fill=1.0,
                                          base=0, pattern=[[-1, P]], channel_multiplier=1))
            step0(nc.gpsimd.memset(blk[:, :], 0.0))
            step0(nc.gpsimd.memset(blk[0:HD, 0:HD], 1.0))
            step0(nc.gpsimd.memset(blk[HD:P, HD:P], 1.0))
            step0(nc.gpsimd.memset(wmask[:, :], 0.0))
            step0(nc.gpsimd.affine_select(out=wmask[:, :], in_=wmask[:, :], compare_op=ALU.is_gt, fill=NEG,
                                          base=0, pattern=[[1, 2 * P]], channel_multiplier=-1))
            step0(nc.gpsimd.affine_select(out=wmask[:, :], in_=wmask[:, :], compare_op=ALU.is_ge, fill=NEG,
                                          base=P, pattern=[[-1, 2 * P]], channel_multiplier=1))
            step0(nc.gpsimd.memset(lmask[:, :, :], 0.0))
            for lv in range(LEVELS):
                L = 1 << lv
                up = lmask[:, lv, :].rearrange("p (b u l) -> p b u l", u=2, l=L)[:, :, 1, :]
                nb = P // (2 * L)
                step0(nc.gpsimd.memset(up, 1.0))
                step0(nc.gpsimd.affine_select(out=up, in_=up, compare_op=ALU.is_ge, fill=0.0, base=0,
                                              pattern=[[-2 * L, nb], [0, L]], channel_multiplier=1))
                step0(nc.gpsimd.affine_select(out=up, in_=up, compare_op=ALU.is_ge, fill=0.0, base=L - 1,
                                              pattern=[[2 * L, nb], [0, L]], channel_multiplier=-1))
            step0(nc.gpsimd.affine_select(out=lmask[:, LEVELS, :], in_=lmask[:, LEVELS, :],
                                          compare_op=ALU.not_equal, fill=1.0, base=0, pattern=[[-1, P]],
                                          channel_multiplier=1))
            step0(nc.gpsimd.memset(scan_keep[:, :], 1.0))
            nc.gpsimd.memset(scan_keep[:, 0:T:P], 0.0).then_inc(s_setup, 1)
            for step in order:
                if step[0] == "H1":
                    hh = step[1]
                    if hh == 0:
                        pool.wait_ge(s_attev, NC)
                        nc.gpsimd.memset(A[:, :], 0.0).then_inc(s_setup, 1)
                    pool.wait_ge(s_sig, 3 * hh + 3)
                    gv = rawg[hh % 2]
                    nc.gpsimd.tensor_tensor(gv[:, :], gv[:, :], DD[0][:, :], ALU.mult).then_inc(s_gm, 1)
                elif step[0] == "H2":
                    hh = step[1]
                    pool.wait_ge(s_eb, 2 * hh + 1)
                    pool.wait_ge(s_kq, 2 * hh + 2)
                    if hh == NH - 1:
                        pool.wait_ge(s_on, 2)
                    nc.gpsimd.tensor_tensor(qi(hh), Q[:, :], DD[0][:, :], ALU.mult).then_inc(s_qi, 1)
                elif step[0] == "LV":
                    _, hh, lv = step
                    L = 1 << lv
                    if lv == 0:
                        pool.wait_ge(s_qi, hh + 1)
                    elif lv == 1:
                        pool.wait_ge(s_kt, 2 * hh + 2)
                    else:
                        pool.wait_ge(s_lvm, 2 * (7 * hh + lv - 1))
                    b4 = B[:, :].rearrange("p (b l) -> p b l", l=2 * L)
                    mid = b4[:, :, L - 1:L].broadcast_to([P, T // (2 * L), 2 * L])
                    nc.gpsimd.tensor_tensor(DD[lv % 2][:, :].rearrange("p (b l) -> p b l", l=2 * L), b4, mid,
                                            ALU.subtract).then_inc(s_lvs, 1)
            pool.wait_ge(s_nrs, 1)
            with pool.Fori(0, FT // 2) as i:
                for j in range(2):
                    for half in range(2):
                        pool.wait_ge(s_silu, 4 * i + (2 * j + half + 1))
                        gv = gate[j][:, half, :]
                        nc.gpsimd.tensor_tensor(gv, gv, nrs[:, half * HALF:(half + 1) * HALF], ALU.mult)\
                            .then_inc(s_gr, 1)

        @block.scalar
        def _(act):
            nc.scalar.preload_act_table_set("natural_log_exp_and_others")
            act.wait_ge(s_g1, 16)
            for k in range(KT):
                act.wait_ge(s_x[k], 16)
                nc.scalar.activation(uhi[:, k, :], x[:, k, :], ACT.Copy, scale=g1[:, k:k + 1]).then_inc(s_uhi, 1)
                if k < 2:
                    act.wait_ge(s_vraw[k], 16)
                    nc.scalar.activation(vhi[0][:, k * VP:(k + 1) * VP], vraw[:, k * VP:(k + 1) * VP], ACT.Copy)\
                        .then_inc(s_vhi, 1)
                if k >= 4:
                    act.wait_ge(s_ss, 2 * (k - 3))
                nc.scalar.activation(sq[:, k % 4, :], x[:, k, :], ACT.Square).then_inc(s_sq, 1)
            act.wait_ge(s_pool0, 2)
            act.wait_ge(s_ss, 2 * KT)
            nc.scalar.activation(rs[:, :], ps[:, 6:8, :], ACT.Ln, scale=1.0 / D, bias=eps).then_inc(s_ln, 1)
            act.wait_ge(s_ln, 1)
            nc.scalar.activation(rs[:, :], rs[:, :], ACT.Exp, scale=-0.5).then_inc(s_rs, 1)
            for i in range(2):
                act.wait_ge(s_vraw[i], 32)
                nc.scalar.activation(vhi[1][:, i * VP:(i + 1) * VP], vraw[:, i * VP:(i + 1) * VP], ACT.Copy)\
                    .then_inc(s_vhi, 1)
            act.wait_ge(s_rt, 1)
            nc.scalar.activation(rtok, ps[:, 6:8, :].rearrange("p b (t c) -> p (b t) c", c=P)[:, :, 0], ACT.Copy)\
                .then_inc(s_rtok, 1)
            act.wait_ge(s_rtok, 1)

            def value_out(g):
                n, t = g // NC, g % NC
                act.wait_ge(s_vmm, g + 1)
                nc.scalar.activation(v[:, t, n * VW:(n + 1) * VW], ps[:, g % 8, 0:VW], ACT.Copy,
                                     scale=rtok[:, t:t + 1]).then_inc(s_vev, 1)

            for g in range(V_FIRST):
                value_out(g)
            for step in order:
                kind = step[0]
                if kind == "W":
                    u = step[1]
                    act.wait_ge(s_wraw[u % 2], 16 * (u // 2 + 1))
                    if u >= 2:
                        act.wait_ge(*unit_used(u - 2))
                    n = 6 * P if N_PROJ + 4 <= u < N_PROJ + 8 else 8 * P
                    nc.scalar.activation(whi[u % 2][:, 0:n], wraw[u % 2][:, 0:n], ACT.Copy).then_inc(s_whi, 1)
                    if u == 1:
                        act.wait_ge(s_lb, 2)
                        nc.scalar.activation(lb_e, lb_e, ACT.Exp).then_inc(s_lbact, 1)
                elif kind == "V":
                    value_out(step[1] * NC + step[2])
                elif kind == "AS":
                    i = step[1]
                    act.wait_ge(s_pev, 2 * i + 2)
                    if i >= 2:
                        act.wait_ge(s_ass, 2 * (i - 1))
                    nc.scalar.activation(asq[:, i % 2, :], kq[:, i, :], ACT.Square).then_inc(s_asq, 1)
                elif kind == "AN":
                    i = step[1]
                    act.wait_ge(s_ass, 2 * i + 2)
                    if i:
                        act.wait_ge(s_an, i)
                    nc.scalar.activation(ars[:, :], ps[:, 3:5, :], ACT.Ln, scale=1.0 / HD, bias=eps)\
                        .then_inc(s_aln, 1)
                    act.wait_ge(s_aln, i + 1)
                    nc.scalar.activation(ars[:, :], ars[:, :], ACT.Exp, scale=-0.5).then_inc(s_ars, 1)
                elif kind == "SC":
                    i = step[1]
                    r, n_keys = i % 3, nk(i)
                    act.wait_ge(s_anm, i + 1)
                    for j in range(GRP):
                        nc.scalar.activation(sc[:, r, j, 0:n_keys], sc[:, r, j, 0:n_keys], ACT.Exp,
                                             bias=nmax[:, 4 * r + j:4 * r + j + 1],
                                             accum_out=rsum[:, 4 * r + j:4 * r + j + 1]).then_inc(s_exp, 1)
                    act.wait_ge(s_asn, i + 1)
                    nc.scalar.activation(esink[:, 4 * r:4 * r + 4], esink[:, 4 * r:4 * r + 4], ACT.Exp)\
                        .then_inc(s_exp, 1)
                elif kind == "TR":
                    i = step[1]
                    if i >= 2:
                        act.wait_ge(s_tr, tr_count(i) - 1)
                        act.wait_ge(s_pv, i)
                        nc.scalar.activation(pT[:, 0, :], ps[:, 5, :], ACT.Copy).then_inc(s_pte0, 1)
                elif kind == "PV":
                    i = step[1]
                    if i % 2 == 1:
                        n = i // 2
                        act.wait_ge(s_pv, i + 1)
                        nc.scalar.activation(att[:, :, n * P:(n + 1) * P],
                                             ps[:, 7, :].rearrange("p (i q) -> p i q", q=P), ACT.Copy)\
                            .then_inc(s_attev, 1)
                elif kind == "H1":
                    hh = step[1]
                    act.wait_ge(s_pev, 2 * (5 + 3 * hh + 3))
                    if hh == 0:
                        act.wait_ge(s_attev, NC)
                    else:
                        act.wait_ge(s_lvm, 14 * hh)
                    nc.scalar.activation(rawf[:, :], rawf[:, :], ACT.Sigmoid).then_inc(s_sig, 1)
                    nc.scalar.activation(DD[1][:, :], rawq[:, :], ACT.Sigmoid).then_inc(s_sig, 1)
                    nc.scalar.activation(DD[0][:, :], rawg[hh % 2][:, :], ACT.Sigmoid).then_inc(s_sig, 1)
                    nc.scalar.preload_act_table_set("natural_log_exp_and_others")
                    act.wait_ge(s_sig, 3 * hh + 1)
                    nc.scalar.activation(B[:, :], rawf[:, :], ACT.Ln, scale=omlb[:, hh:hh + 1],
                                         bias=lb[:, hh:hh + 1]).then_inc(s_lnf, 1)
                elif kind == "H2":
                    hh = step[1]
                    act.wait_ge(s_scan, hh + 1)
                    act.wait_ge(s_gm, hh + 1)
                    nc.scalar.activation(DD[0][:, :], B[:, :], ACT.Exp).then_inc(s_eb, 1)
                    if hh >= 2:
                        act.wait_ge(s_st, NC * (hh - 1))
                    nc.scalar.activation(ebt[:, 8 * (hh % 2):8 * (hh % 2) + 8], B[:, P - 1:T:P], ACT.Exp)\
                        .then_inc(s_eb, 1)
                    act.wait_ge(s_d2, hh + 1)
                    nc.scalar.activation(DD[1][:, :], DD[1][:, :], ACT.Exp).then_inc(s_e2, 1)
                elif kind == "KE":
                    hh = step[1]
                    for x2 in range(2):
                        act.wait_ge(s_kt, 2 * hh + x2 + 1)
                        if hh and not x2:
                            act.wait_ge(s_oc, NC * hh)
                        nc.scalar.activation(KDT[:, 4 * x2:4 * x2 + 4, :], ps[:, 3 + x2, :], ACT.Copy)\
                            .then_inc(s_kte, 1)
                elif kind == "LV":
                    _, hh, lv = step
                    L = 1 << lv
                    act.wait_ge(s_lvs, 7 * hh + lv + 1)
                    dv = DD[lv % 2][:, :].rearrange("p (b u l) -> p b u l", u=2, l=L)
                    nc.scalar.activation(dv[:, :, 0, :], dv[:, :, 0, :], ACT.Exp, scale=-1.0).then_inc(s_lve, 1)
                    nc.scalar.activation(dv[:, :, 1, :], dv[:, :, 1, :], ACT.Exp).then_inc(s_lve, 1)
                elif kind == "OC":
                    _, hh, c = step
                    if c % 4 == 3:
                        x2 = c // 4
                        act.wait_ge(s_oc, NC * hh + c + 1)
                        nc.scalar.activation(rec[:, hh, x2 * HALF:(x2 + 1) * HALF], ps[:, 5 + x2, :], ACT.Copy)\
                            .then_inc(s_oev, 1)
                elif kind == "OS":
                    hh = step[1]
                    act.wait_ge(s_oev, 2 * hh + 2)
                    if hh:
                        act.wait_ge(*((s_on1, hh), (s_kq, 2 * NH - 1), (s_lmm, 16 * NH))[hh - 1])
                    nc.scalar.activation(on_tmp(hh)[:, :], rec[:, hh, :], ACT.Square).then_inc(s_osq, 1)
                elif kind == "ON":
                    hh = step[1]
                    act.wait_ge(s_oss, 2 * hh + 2)
                    nc.scalar.activation(on_tmp(hh)[:, :], ps[:, 5:7, :], ACT.Ln, scale=1.0 / P, bias=eps)\
                        .then_inc(s_oln, 1)
                    act.wait_ge(s_oln, hh + 1)
                    nc.scalar.activation(on_tmp(hh)[:, :], on_tmp(hh)[:, :], ACT.Exp, scale=-0.5).then_inc(s_ors, 1)
                elif kind == "MS":
                    i = step[1]
                    if i < 4:
                        act.wait_ge(s_pmm, 2 * N_PROJ)
                        dst, src = mhi0[:, i, :], att[:, i, :]
                    else:
                        act.wait_ge(s_on, i - 3)
                        act.wait_ge(s_mlo, 4)
                        src = rec[:, i - 4, :]
                        dst = mhi1[:, i - 4, :] if i < 7 else mhi3[:, :]
                    nc.scalar.activation(dst, src, ACT.Copy).then_inc(s_mhi, 1)
                elif kind == "N2":
                    m = step[1]
                    act.wait_ge(s_oadd, 32 + 2 * m + 2)
                    nc.scalar.activation(u2hi[:, m, :], h[:, m, :], ACT.Copy, scale=g2[:, m:m + 1])\
                        .then_inc(s_u2hi, 1)
                    if m >= 2:
                        act.wait_ge(s_nss, 2 * (m - 1))
                    nc.scalar.activation(nsq[:, m % 2, :], h[:, m, :], ACT.Square).then_inc(s_nsq, 1)
                    if m == KT - 1:
                        act.wait_ge(s_nss, 2 * KT)
                        for half in range(2):
                            nc.scalar.activation(nrs[:, half * HALF:(half + 1) * HALF], ps[:, (2, 7)[half], :], ACT.Ln,
                                                 scale=1.0 / D, bias=eps).then_inc(s_nln, 1)
                        act.wait_ge(s_nln, 2)
                        nc.scalar.activation(nrs[:, :], nrs[:, :], ACT.Exp, scale=-0.5).then_inc(s_nrs, 1)
                elif kind == "F":
                    p = step[1]
                    act.wait_ge(s_fraw[p], 16)
                    act.wait_ge(*((s_on, 3), (s_lmm, 64), (s_lmm, 64), (s_oc, 32), (s_on, 4), (s_omm, 48))[p])
                    nc.scalar.activation(fhi[p][:, :], fraw[p][:, :], ACT.Copy).then_inc(s_fhi, 1)

            def ffn(i, last):
                for j in range(2):
                    for half in range(2):
                        act.wait_ge(s_gsc, 4 * i + (2 * j + half + 1))
                        nc.scalar.activation(gate[j][:, half, :], gate[j][:, half, :], ACT.Silu).then_inc(s_silu, 1)
                    for half in range(2):
                        act.wait_ge(s_hid, 4 * i + (2 * j + half + 1))
                        nc.scalar.activation(hidhi[:, j, half * HALF:(half + 1) * HALF], hid[:, half, :], ACT.Copy)\
                            .then_inc(s_hhi, 1)
                    for p in () if last else (2 * j, 2 * j + 1):
                        act.wait_ge(s_fraw[p], 16 * i + 32)
                        act.wait_ge(s_fmm, 8 * i + (2 * p + 2))
                        nc.scalar.activation(fhi[p][:, :], fraw[p][:, :], ACT.Copy).then_inc(s_fhi, 1)
                for p in () if last else (4, 5):
                    act.wait_ge(s_fraw[p], 16 * i + 32)
                    act.wait_ge(s_dmm, 16 * i + 16)
                    nc.scalar.activation(fhi[p][:, :], fraw[p][:, :], ACT.Copy).then_inc(s_fhi, 1)

            with act.Fori(0, FT // 2 - 1) as i:
                ffn(i, False)
            ffn(FT // 2 - 1, True)

        @block.tensor
        def _(pe):
            def three(out, whi_, wlo_, xhi_, xlo_, first, last):
                nc.tensor.matmul(out, whi_, xhi_, start=first, stop=False)
                nc.tensor.matmul(out, whi_, xlo_, start=False, stop=False)
                return nc.tensor.matmul(out, wlo_, xhi_, start=False, stop=last)

            def value_part(g, k):
                n, t = g // NC, g % NC
                tok, w = slice(t * P, (t + 1) * P), slice(k * VW, (k + 1) * VW)
                return three(ps[:, g % 8, 0:VW], uhi[:, k, tok], ulo[:, k, tok], vhi[n][:, w], vlo[n][:, w],
                             k == 0, k == KT - 1)

            pe.wait_ge(s_pool0, 2)
            for k in range(KT):
                pe.wait_ge(s_ulo, k + 1)
                if k % 4 == 0:
                    pe.wait_ge(s_vlo, k // 4 + 1)
                for g in range(V_FIRST):
                    mm = value_part(g, k)
                    if k == KT - 1:
                        mm.then_inc(s_vmm, 1)
                for q in (2 * k, 2 * k + 1) if k < 4 else ():
                    pe.wait_ge(s_sq, q + 1)
                    for half in range(2):
                        nc.tensor.matmul(ps[:, 6 + half, :], ones[:, :], sq[:, q % 4, half * HALF:(half + 1) * HALF],
                                         start=(q == 0), stop=(q == KT - 1)).then_inc(s_ss, 1)
                if k == 6:
                    pe.wait_ge(s_rs, 1)
                    pe.wait_ge(s_setup, 1)
                    for t in range(NC):
                        mm = nc.tensor.transpose(ps[:, 6 + t // 4, (t % 4) * P:(t % 4 + 1) * P],
                                                 rs[:, t * P:(t + 1) * P], ident[:, :])
                    mm.then_inc(s_rt, 1)
            for step in order:
                kind = step[0]
                if kind == "V":
                    _, n, t = step
                    g = n * NC + t
                    if g == V_FIRST:
                        pe.wait_ge(s_rtok, 1)
                    if g >= NC:
                        pe.wait_ge(s_vev, g - 7)
                    for k in range(KT):
                        if g == NC and k % 4 == 0:
                            pe.wait_ge(s_vlo, 2 + k // 4 + 1)
                        mm = value_part(g, k)
                    mm.then_inc(s_vmm, 1)
                elif kind == "P":
                    _, g, part = step
                    u, half = g // 2, g % 2
                    if part == 0:
                        pe.wait_ge(*((s_vev, NC + g + 1) if g < 3 else (s_pev, g - 2)))
                        pe.wait_ge(s_wlo, u + 1)
                    for k in (2 * part, 2 * part + 1):
                        w = slice(k * P, (k + 1) * P)
                        t = slice(half * HALF, (half + 1) * HALF)
                        mm = three(ps[:, g % 3, :], whi[u % 2][:, w], wlo[u % 2][:, w], uhi[:, k, t],
                                   ulo[:, k, t], k == 0, k == KT - 1)
                    if part == 3:
                        mm.then_inc(s_pmm, 1)
                elif kind == "O":
                    _, g, part = step
                    grp, m, half = g // 16, g % 16 // 2, g % 2
                    u = N_PROJ + g // 4 if grp < 2 else N_UNITS - 1
                    n_k = (4, 3, 1)[grp]
                    if part == 0:
                        if g < 3:
                            pe.wait_ge(s_pev, 2 * N_PROJ + g - 2)
                        elif g < 32:
                            pe.wait_ge(s_oadd, g - 2)
                        else:
                            pe.wait_ge(s_oadd, g - 2 if g < 34 else g - 1)
                        pe.wait_ge(s_wlo, u + 1)
                    for k in range(2 * part, min(2 * part + 2, n_k)):
                        if g % 16 == 0:
                            pe.wait_ge(s_mlo, (0, 4, 7)[grp] + k + 1)
                        w0 = m * P if grp == 2 else (m % 2 * n_k + k) * P
                        w, t = slice(w0, w0 + P), slice(half * HALF, (half + 1) * HALF)
                        mhi, mlo = ((mhi0[:, k, t], mlo0[:, k, t]) if grp == 0 else
                                    (mhi1[:, k, t], mlo1[:, k, t]) if grp == 1 else (mhi3[:, t], mlo3[:, t]))
                        mm = three(ps[:, out_bank(g), :], whi[u % 2][:, w], wlo[u % 2][:, w], mhi, mlo,
                                   k == 0, k == n_k - 1)
                    if k == n_k - 1:
                        mm.then_inc(s_omm, 1)
                elif kind == "AM":
                    i = step[1]
                    pe.wait_ge(s_asq, i + 1)
                    if i == 0:
                        pe.wait_ge(s_vev, 2 * NC)
                    else:
                        pe.wait_ge(s_aln, i)
                    for half in range(2):
                        nc.tensor.matmul(ps[:, 3 + half, :], blk[:, :], asq[:, i % 2, half * HALF:(half + 1) * HALF],
                                         start=True, stop=True).then_inc(s_ass, 1)
                elif kind == "SC":
                    i = step[1]
                    n, g = i // 2, i % 2
                    if i == 0:
                        pe.wait_ge(s_an, 5)
                    else:
                        pe.wait_ge(s_masked, i)
                    rows = slice(HD * g, HD * g + HD)
                    for j in range(GRP):
                        mm = nc.tensor.matmul(ps[:, 3 + j // 2, (j % 2) * 2 * P:(j % 2) * 2 * P + nk(i)],
                                              kq[rows, 1 + j, n * P:(n + 1) * P],
                                              kq[rows, 0, (n + 1) * P - nk(i):(n + 1) * P], start=True, stop=True)
                    mm.then_inc(s_scm, 1)
                elif kind == "TR":
                    i = step[1]
                    pe.wait_ge(s_prob, i + 1)
                    for b in range(nk(i) // P):
                        cur = b == nk(i) // P - 1
                        if cur and i:
                            pe.wait_ge(s_pte1, i)
                        if not cur and i > 2:
                            pe.wait_ge(s_pte0, i - 2)
                        for j in range(GRP):
                            mm = nc.tensor.transpose(ps[:, 6 if cur else 5, j * P:(j + 1) * P],
                                                     sc[:, i % 3, j, b * P:(b + 1) * P], ident[:, :])
                        mm.then_inc(s_tr, 1)
                elif kind == "PV":
                    i = step[1]
                    n, g = i // 2, i % 2
                    if g == 0 and n:
                        pe.wait_ge(s_attev, n)
                    if n:
                        pe.wait_ge(s_pte0, i - 1)
                    pe.wait_ge(s_pte1, i + 1)
                    out = ps[HD * g:HD * g + HD, 7, :]
                    vc = slice(NH * P + HD * g, NH * P + HD * g + HD)
                    if n:
                        nc.tensor.matmul(out, v[:, n - 1, vc], pT[:, 0, :], start=True, stop=False)
                    nc.tensor.matmul(out, v[:, n, vc], pT[:, 1, :], start=(n == 0), stop=True).then_inc(s_pv, 1)
                elif kind == "KT":
                    hh = step[1]
                    pe.wait_ge(s_kd, hh + 1)
                    if hh:
                        pe.wait_ge(s_cp, 16 * hh)
                    for c in range(NC):
                        mm = nc.tensor.transpose(ps[:, 3 + c // 4, (c % 4) * P:(c % 4 + 1) * P],
                                                 DD[1][:, c * P:(c + 1) * P], ident[:, :])
                        if c % 4 == 3:
                            mm.then_inc(s_kt, 1)
                elif kind == "LM":
                    _, hh, lv = step
                    if lv < LEVELS:
                        pe.wait_ge(s_lvm, 2 * (7 * hh + lv + 1))
                        lhs = rhs = M[lv % 2]
                    else:
                        lhs, rhs = K, Q
                    if lv == 0:
                        pe.wait_ge(s_kte, 2 * hh + 2)
                    for c in range(NC):
                        done = 2 * (8 * hh + lv - 1) + c // 4 + 1
                        if c % 4 == 0 and lv:
                            pe.wait_ge(s_cp, done)
                        cs = slice(c * P, (c + 1) * P)
                        mm = nc.tensor.matmul(ps[:, 3 + c // 4, (c % 4) * P:(c % 4 + 1) * P], lhs[:, cs], rhs[:, cs],
                                              start=True, stop=True)
                        if c % 4 == 3:
                            mm.then_inc(s_lmm, 1)
                elif kind == "OC":
                    _, hh, c = step
                    if c == 0:
                        pe.wait_ge(s_cp, 16 * (hh + 1))
                        pe.wait_ge(s_qi, hh + 1)
                        pe.wait_ge(*((s_oln, hh) if hh else (s_attev, NC)))
                    if c or hh:
                        pe.wait_ge(s_st, NC * hh + c)
                    cs = slice(c * P, (c + 1) * P)
                    vh = v[:, c, hh * P:(hh + 1) * P]
                    out = ps[:, 5 + c // 4, (c % 4) * P:(c % 4 + 1) * P]
                    nc.tensor.matmul(ps[:, 7, (c % 4) * P:(c % 4 + 1) * P], KDT[:, c, :], vh, start=True, stop=True)
                    mm = nc.tensor.matmul(out, vh, A[:, cs], start=True, stop=(c == 0))
                    if c:
                        mm = nc.tensor.matmul(out, S[:, c % 2, :], qi(hh)[:, cs], start=False, stop=True)
                    mm.then_inc(s_oc, 1)
                elif kind == "OM":
                    hh = step[1]
                    pe.wait_ge(s_osq, hh + 1)
                    for half in range(2):
                        nc.tensor.matmul(ps[:, 5 + half, :], ones[:, :],
                                         on_tmp(hh)[:, half * HALF:(half + 1) * HALF],
                                         start=True, stop=True).then_inc(s_oss, 1)
                elif kind == "N2":
                    m = step[1]
                    pe.wait_ge(s_nsq, m + 1)
                    if m == 0:
                        pe.wait_ge(s_oadd, 32)
                        pe.wait_ge(s_st, NH * NC)
                    for half in range(2):
                        nc.tensor.matmul(ps[:, (2, 7)[half], :], ones[:, :], nsq[:, m % 2, half * HALF:(half + 1) * HALF],
                                         start=(m == 0), stop=(m == KT - 1)).then_inc(s_nss, 1)
                    pe.wait_ge(s_u2lo, m + 1)
                    for p in range(2):
                        if m == 0:
                            pe.wait_ge(s_flo, p + 1)
                        for half in range(2):
                            w, t = slice(m * P, (m + 1) * P), slice(half * HALF, (half + 1) * HALF)
                            mm = three(ps[:, ffn_bank(True, p, half), :], fhi[p][:, w], flo[p][:, w],
                                       u2hi[:, m, t], u2lo[:, m, t], m == 0, m == KT - 1)
                            if m == KT - 1:
                                mm.then_inc(s_fmm, 1)

            def ffn(i, first):
                for p in range(2 if first else 0, 4):
                    pe.wait_ge(s_flo, 6 * i + (p + 1))
                    for half in range(2):
                        t = slice(half * HALF, (half + 1) * HALF)
                        if first:
                            pe.wait_ge(*((s_oadd, 48) if p == 2 else (s_nln, half + 1)))
                        elif p < 2:
                            pe.wait_ge(s_dadd, 16 * i + (2 * p + half - 3))
                        else:
                            pe.wait_ge((s_gsc, s_hid)[p - 2], 4 * i + (half - 1))
                        for k in range(KT):
                            w = slice(k * P, (k + 1) * P)
                            mm = three(ps[:, ffn_bank(first, p, half), :], fhi[p][:, w], flo[p][:, w], u2hi[:, k, t],
                                       u2lo[:, k, t], k == 0, k == KT - 1)
                        mm.then_inc(s_fmm, 1)
                for q in range(4):
                    for j in range(2):
                        if q == 0:
                            pe.wait_ge(s_flo, 6 * i + (4 + j + 1))
                            pe.wait_ge(s_hlo, 4 * i + (2 * j + 2))
                        for b in range(4):
                            m, half = 2 * q + b // 2, b % 2
                            if j == 0 and q:
                                pe.wait_ge(s_dadd, 16 * i + (4 * (q - 1) + b + 1))
                            w = slice(m * P, (m + 1) * P)
                            t = slice(half * HALF, (half + 1) * HALF)
                            mm = three(ps[:, (3 if first else 0) + b, :], fhi[4 + j][:, w], flo[4 + j][:, w],
                                       hidhi[:, j, t], hidlo[:, j, t], j == 0, j == 1)
                            if j:
                                mm.then_inc(s_dmm, 1)

            ffn(0, True)
            with pe.Fori(1, FT // 2) as i:
                ffn(i, False)

        @block.vector
        def _(dve):
            def ffn_weights_lo(p, n):
                dve.wait_ge(s_fhi, n)
                nc.vector.tensor_tensor(flo[p][:, :], fraw[p][:, :], fhi[p][:, :].bitcast(F32), ALU.subtract)\
                    .then_inc(s_flo, 1)

            def value_weights_lo(n, i):
                c = slice(i * VP, (i + 1) * VP)
                dve.wait_ge(s_vhi, 2 * n + i + 1)
                nc.vector.tensor_tensor(vlo[n][:, c], vraw[:, c], vhi[n][:, c].bitcast(F32), ALU.subtract)\
                    .then_inc(s_vlo, 1)

            for k in range(KT):
                dve.wait_ge(s_uhi, k + 1)
                nc.vector.scalar_tensor_tensor(ulo[:, k, :], x[:, k, :], g1[:, k:k + 1], uhi[:, k, :].bitcast(F32),
                                               ALU.mult, ALU.subtract).then_inc(s_ulo, 1)
                if k < 2:
                    value_weights_lo(0, k)
            dve.wait_ge(s_const, 16 * N_CONST)
            nc.vector.tensor_tensor(lb_m, lb_in[:, 0:4], lb_in[:, 4:8], ALU.max).then_inc(s_lb, 1)
            dve.wait_ge(s_lb, 1)
            nc.vector.tensor_tensor(lb_e.rearrange("p (r h) -> p r h", r=2), lb_in.rearrange("p (r h) -> p r h", r=2),
                                    lb_m.unsqueeze(1).broadcast_to([P, 2, 4]), ALU.subtract).then_inc(s_lb, 1)
            nc.vector.tensor_scalar(nsink, sink, -1.0, None, ALU.mult)
            nc.vector.tensor_scalar(qg, qg, HD ** -0.5, None, ALU.mult)
            value_weights_lo(1, 0)
            value_weights_lo(1, 1)
            for step in order:
                kind = step[0]
                if kind == "W":
                    u = step[1]
                    dve.wait_ge(s_whi, u + 1)
                    n = 6 * P if N_PROJ + 4 <= u < N_PROJ + 8 else 8 * P
                    nc.vector.tensor_tensor(wlo[u % 2][:, 0:n], wraw[u % 2][:, 0:n], whi[u % 2][:, 0:n].bitcast(F32),
                                            ALU.subtract).then_inc(s_wlo, 1)
                    if u == 1:
                        dve.wait_ge(s_lbact, 1)
                        nc.vector.tensor_tensor(lb_s, lb_e[:, 0:4], lb_e[:, 4:8], ALU.add).then_inc(s_lb, 1)
                        dve.wait_ge(s_lb, 3)
                        nc.vector.reciprocal(lb_s, lb_s).then_inc(s_lb, 1)
                        dve.wait_ge(s_lb, 4)
                        nc.vector.tensor_tensor(lb, lb_e[:, 0:4], lb_s, ALU.mult).then_inc(s_lb, 1)
                        nc.vector.tensor_tensor(omlb, lb_e[:, 4:8], lb_s, ALU.mult).then_inc(s_lb, 1)
                        dve.wait_ge(s_lb, 6)
                        nc.vector.tensor_scalar(nomlb, omlb, -1.0, None, ALU.mult).then_inc(s_lb, 1)
                        nc.vector.tensor_scalar(lb, lb, TINY, None, ALU.max).then_inc(s_lb, 1)
                elif kind == "P" and step[2] == 3:
                    g = step[1]
                    u, half = g // 2, g % 2
                    cols = slice(half * HALF, (half + 1) * HALF)
                    dve.wait_ge(s_pmm, g + 1)
                    if g == 0:
                        dve.wait_ge(s_rs, 1)
                    if u < 5:
                        dst = kq[:, u, cols]
                    else:
                        hh, j = divmod(u - 5, 3)
                        dst = (rawf, rawq, rawg[hh % 2])[j][:, cols]
                        if j == 0 and hh:
                            dve.wait_ge(s_lnf, hh)
                    nc.vector.tensor_tensor(dst, ps[:, g % 3, :], rs[:, cols], ALU.mult).then_inc(s_pev, 1)
                elif kind == "O" and step[2] == (1, 1, 0)[step[1] // 16]:
                    g = step[1]
                    m, half = g % 16 // 2, g % 2
                    dve.wait_ge(s_omm, g + 1)
                    if g < 16:
                        dve.wait_ge(s_x[m], 32)
                    else:
                        dve.wait_ge(s_oadd, g - 15)
                    hv = h[:, m, half * HALF:(half + 1) * HALF]
                    nc.vector.tensor_tensor(hv, ps[:, out_bank(g), :], hv, ALU.add).then_inc(s_oadd, 1)
                elif kind == "AN":
                    i = step[1]
                    dve.wait_ge(s_ars, i + 1)
                    nc.vector.scalar_tensor_tensor(kq[:, i, :], kq[:, i, :], qg if i else kg, ars[:, :],
                                                   ALU.mult, ALU.mult).then_inc(s_an, 1)
                elif kind == "SC":
                    i = step[1]
                    r, g, n_keys = i % 3, i % 2, nk(i)
                    dve.wait_ge(s_scm, i + 1)
                    if i >= 3:
                        dve.wait_ge(s_tr, tr_count(i - 3))
                    sv = sc[:, r, :, 0:n_keys]
                    pv = ps[:, 3:5, :].rearrange("p b (j n) -> p (b j) n", j=2)[:, :, 0:n_keys]
                    mv = wmask[:, 2 * P - n_keys:2 * P].unsqueeze(1).broadcast_to([P, GRP, n_keys])
                    nc.vector.tensor_tensor(sv, pv, mv, ALU.add).then_inc(s_masked, 1)
                    dve.wait_ge(s_masked, i + 1)
                    nm = nmax[:, 4 * r:4 * r + 4]
                    nc.vector.tensor_reduce(nm, sv, AX.X, ALU.max, negate=True).then_inc(s_amx, 1)
                    dve.wait_ge(s_amx, i + 1)
                    nc.vector.tensor_tensor(nm, nm, nsink[:, GRP * g:GRP * g + GRP], ALU.min).then_inc(s_anm, 1)
                    dve.wait_ge(s_anm, i + 1)
                    nc.vector.tensor_tensor(esink[:, 4 * r:4 * r + 4], nm, sink[:, GRP * g:GRP * g + GRP], ALU.add)\
                        .then_inc(s_asn, 1)
                elif kind == "SN":
                    i = step[1]
                    r, n_keys = i % 3, nk(i)
                    q4 = slice(4 * r, 4 * r + 4)
                    dve.wait_ge(s_exp, 5 * (i + 1))
                    nc.vector.tensor_tensor(den[:, q4], rsum[:, q4], esink[:, q4], ALU.add).then_inc(s_den, 1)
                    dve.wait_ge(s_den, i + 1)
                    nc.vector.reciprocal(rden[:, q4], den[:, q4]).then_inc(s_rden, 1)
                    dve.wait_ge(s_rden, i + 1)
                    for j in range(GRP):
                        ins = nc.vector.tensor_scalar(sc[:, r, j, 0:n_keys], sc[:, r, j, 0:n_keys],
                                                      rden[:, 4 * r + j:4 * r + j + 1], None, ALU.mult)
                    ins.then_inc(s_prob, 1)
                elif kind == "TR":
                    i = step[1]
                    dve.wait_ge(s_tr, tr_count(i))
                    if i:
                        dve.wait_ge(s_pv, i)
                    nc.vector.tensor_copy(pT[:, 1, :], ps[:, 6, :]).then_inc(s_pte1, 1)
                elif kind == "H1":
                    hh = step[1]
                    dve.wait_ge(s_sig, 3 * hh + 1)
                    if hh:
                        dve.wait_ge(s_lmm, 16 * hh)
                    nc.vector.tensor_scalar(K[:, :], rawf[:, :], nomlb[:, hh:hh + 1], omlb[:, hh:hh + 1],
                                            ALU.mult, ALU.add).then_inc(s_kq, 1)
                    dve.wait_ge(s_sig, 3 * hh + 2)
                    nc.vector.scalar_tensor_tensor(Q[:, :], rawq[:, :], P ** -0.5, DD[1][:, :], ALU.mult, ALU.mult)\
                        .then_inc(s_kq, 1)
                    dve.wait_ge(s_lnf, hh + 1)
                    nc.vector.tensor_tensor_scan(B[:, :], scan_keep[:, :], B[:, :], 0.0, ALU.mult, ALU.add)\
                        .then_inc(s_scan, 1)
                elif kind == "H2":
                    hh = step[1]
                    dve.wait_ge(s_scan, hh + 1)
                    dve.wait_ge(s_kq, 2 * hh + 2)
                    bc = B[:, :].rearrange("p (c t) -> p c t", t=P)
                    dv = DD[1][:, :].rearrange("p (c t) -> p c t", t=P)
                    nc.vector.tensor_tensor(dv, bc[:, :, P - 1:P].broadcast_to([P, NC, P]), bc, ALU.subtract)\
                        .then_inc(s_d2, 1)
                    dve.wait_ge(s_e2, hh + 1)
                    nc.vector.tensor_tensor(DD[1][:, :], K[:, :], DD[1][:, :], ALU.mult).then_inc(s_kd, 1)
                elif kind == "LV":
                    _, hh, lv = step
                    L = 1 << lv
                    dve.wait_ge(s_lve, 2 * (7 * hh + lv + 1))
                    if lv >= 2:
                        dve.wait_ge(s_lmm, 2 * (8 * hh + lv - 1))
                    for up, src in ((0, K), (1, Q)):
                        mv, sv, ev = (a[:, :].rearrange("p (b u l) -> p b u l", u=2, l=L)[:, :, up, :]
                                      for a in (M[lv % 2], src, DD[lv % 2]))
                        nc.vector.tensor_tensor(mv, sv, ev, ALU.mult).then_inc(s_lvm, 1)
                elif kind == "LM":
                    _, hh, lv = step
                    for x2 in range(2):
                        dve.wait_ge(s_lmm, 2 * (8 * hh + lv) + x2 + 1)
                        if lv == 0 and x2 == 0:
                            dve.wait_ge(*((s_oc, NC * hh) if hh else (s_setup, 2)))
                        if lv:
                            dve.wait_ge(s_cp, 2 * (8 * hh + lv - 1) + x2 + 1)
                        av = A[:, x2 * HALF:(x2 + 1) * HALF].rearrange("p (c t) -> p c t", t=P)
                        nc.vector.copy_predicated(av, lmask[:, lv, :].unsqueeze(1).broadcast_to([P, 4, P]),
                                                  ps[:, 3 + x2, :].rearrange("p (c t) -> p c t", t=P))\
                            .then_inc(s_cp, 1)
                elif kind == "OC":
                    _, hh, c = step
                    dve.wait_ge(s_oc, NC * hh + c + 1)
                    st = ps[:, 7, (c % 4) * P:(c % 4 + 1) * P]
                    if c:
                        dve.wait_ge(s_st, NC * hh + c)
                        nc.vector.scalar_tensor_tensor(S[:, (c + 1) % 2, :], S[:, c % 2, :], ebt[:, 8 * (hh % 2) + c:8 * (hh % 2) + c + 1], st,
                                                       ALU.mult, ALU.add).then_inc(s_st, 1)
                    else:
                        dve.wait_ge(s_eb, 2 * hh + 2)
                        nc.vector.tensor_copy(S[:, 1, :], st).then_inc(s_st, 1)
                elif kind == "ON":
                    hh = step[1]
                    dve.wait_ge(s_ors, hh + 1)
                    nc.vector.scalar_tensor_tensor(rec[:, hh, :], rec[:, hh, :], og, on_tmp(hh)[:, :],
                                                   ALU.mult, ALU.mult).then_inc(s_on1, 1)
                    dve.wait_ge(s_on1, hh + 1)
                    dve.wait_ge(s_gm, hh + 1)
                    nc.vector.tensor_tensor(rec[:, hh, :], rec[:, hh, :], rawg[hh % 2][:, :], ALU.mult)\
                        .then_inc(s_on, 1)
                elif kind == "MS":
                    i = step[1]
                    dve.wait_ge(s_mhi, i + 1)
                    if i < 4:
                        dst, src, hi = mlo0[:, i, :], att[:, i, :], mhi0[:, i, :]
                    elif i < 7:
                        dst, src, hi = mlo1[:, i - 4, :], rec[:, i - 4, :], mhi1[:, i - 4, :]
                    else:
                        dst, src, hi = mlo3[:, :], rec[:, 3, :], mhi3[:, :]
                    nc.vector.tensor_tensor(dst, src, hi.bitcast(F32), ALU.subtract).then_inc(s_mlo, 1)
                elif kind == "N2":
                    m = step[1]
                    dve.wait_ge(s_u2hi, m + 1)
                    nc.vector.scalar_tensor_tensor(u2lo[:, m, :], h[:, m, :], g2[:, m:m + 1],
                                                   u2hi[:, m, :].bitcast(F32), ALU.mult, ALU.subtract)\
                        .then_inc(s_u2lo, 1)
                elif kind == "F":
                    ffn_weights_lo(step[1], step[1] + 1)
            def ffn(i, first, last):
                for j in range(2):
                    for half in range(2):
                        dve.wait_ge(s_fmm, 8 * i + (4 * j + half + 1))
                        if first and not j and not half:
                            dve.wait_ge(s_nrs, 1)
                        nc.vector.tensor_tensor(gate[j][:, half, :], ps[:, ffn_bank(first, 2 * j, half), :],
                                                nrs[:, half * HALF:(half + 1) * HALF], ALU.mult).then_inc(s_gsc, 1)
                    for half in range(2):
                        r = 2 * j + half
                        dve.wait_ge(s_fmm, 8 * i + (4 * j + 2 + half + 1))
                        dve.wait_ge(s_gr, 4 * i + (r + 1))
                        nc.vector.tensor_tensor(hid[:, half, :], ps[:, ffn_bank(first, 2 * j + 1, half), :],
                                                gate[j][:, half, :], ALU.mult).then_inc(s_hid, 1)
                    for half in range(2):
                        r = 2 * j + half
                        dve.wait_ge(s_hhi, 4 * i + (r + 1))
                        t = slice(half * HALF, (half + 1) * HALF)
                        nc.vector.tensor_tensor(hidlo[:, j, t], hid[:, half, :], hidhi[:, j, t].bitcast(F32),
                                                ALU.subtract).then_inc(s_hlo, 1)
                    for p in () if last else (2 * j, 2 * j + 1):
                        ffn_weights_lo(p, 6 * i + (6 + p + 1))
                for g in range(16):
                    m, half = g // 2, g % 2
                    dve.wait_ge(s_dmm, 16 * i + (g + 1))
                    if not first:
                        dve.wait_ge(s_dadd, 16 * i + (-16 + g + 1))
                    hv = h[:, m, half * HALF:(half + 1) * HALF]
                    nc.vector.tensor_tensor(hv, ps[:, (3 if first else 0) + g % 4, :], hv, ALU.add)\
                        .then_inc(s_dadd, 1)
                for p in () if last else (4, 5):
                    ffn_weights_lo(p, 6 * i + (6 + p + 1))

            ffn(0, True, False)
            with dve.Fori(1, FT // 2 - 1) as i:
                ffn(i, False, False)
            ffn(FT // 2 - 1, False, True)


def kernel(x, norm1_gain, w_in, hgrn_lb_logits, hgrn_out_gain, q_norm_gain, k_norm_gain, attn_sinks, w_out,
           norm2_gain, w_ffn_gate, w_ffn_up, w_ffn_down):
    import numpy as np
    import concourse.bacc as bacc
    from concourse.bass_utils import run_bass_kernel_spmd

    def tiles(w):
        k, n = w.shape
        return w.reshape(k // P, P, n // P, P).transpose(2, 1, 0, 3).reshape(n // P, P, k)

    w = np.asarray(w_in)[0]
    hw = NH * P
    hq, hf, hi, hg = (w[:, i * hw:(i + 1) * hw] for i in range(4))
    aq = w[:, 4 * hw:4 * hw + AH * HD]
    ak, av = (w[:, 4 * hw + AH * HD + i * P:4 * hw + AH * HD + (i + 1) * P] for i in range(2))
    q_tiles = [np.concatenate([aq[:, i * HD:(i + 1) * HD], aq[:, (i + GRP) * HD:(i + GRP + 1) * HD]], 1)
               for i in range(GRP)]
    cols = [ak] + q_tiles
    for i in range(NH):
        cols += [a[:, i * P:(i + 1) * P] for a in (hf, hq, hg)]
    wproj = tiles(np.concatenate(cols, 1))
    wv = np.concatenate([hi, av], 1).reshape(KT, P, 2, VW).transpose(2, 1, 0, 3).reshape(2, P, KT * VW)
    wo = np.asarray(w_out)[0]
    ao = wo[hw:]
    att_rows = [np.concatenate([ao[i * HD:(i + 1) * HD], ao[(i + GRP) * HD:(i + GRP + 1) * HD]], 0)
                for i in range(GRP)]

    def pairs(rows):
        k = rows.shape[0]
        return tiles(rows).reshape(4, 2, P, k).transpose(0, 2, 1, 3).reshape(4, P, 2 * k)

    qg, kg = (np.concatenate([np.asarray(a)[0], np.asarray(a)[0]]).reshape(P, 1) for a in (q_norm_gain, k_norm_gain))
    arrays = {
        "xT": np.asarray(x)[0].T,
        "wv": wv,
        "wproj": wproj,
        "wo_a": pairs(np.concatenate(att_rows, 0)),
        "wo_b": pairs(wo[:3 * P]),
        "wo_c": wo[3 * P:hw],
        "wg": tiles(np.asarray(w_ffn_gate)[0]),
        "wu": tiles(np.asarray(w_ffn_up)[0]),
        "wd": np.asarray(w_ffn_down)[0].reshape(FT, P, D),
        "gain1": np.asarray(norm1_gain)[0].reshape(KT, P).T,
        "gain2": np.asarray(norm2_gain)[0].reshape(KT, P).T,
        "lbl": np.asarray(hgrn_lb_logits).reshape(2, NH, P).transpose(2, 0, 1).reshape(P, 2 * NH),
        "ogain": np.asarray(hgrn_out_gain)[0].reshape(P, 1),
        "qgain": qg,
        "kgain": kg,
        "sinks": np.broadcast_to(np.asarray(attn_sinks)[0], (P, AH)),
    }
    arrays = {n: np.ascontiguousarray(a) for n, a in arrays.items()}
    nc = bacc.Bacc("TRN2", target_bir_lowering=False, num_devices=1)
    args = [nc.dram_tensor(n, a.shape, mybir.dt.from_np(a.dtype), kind="ExternalInput").ap()
            for n, a in arrays.items()]
    y = nc.dram_tensor("yT", (D, T), F32, kind="ExternalOutput").ap()
    build(nc, *args, y)
    r = run_bass_kernel_spmd(nc, [arrays], core_ids=[0])
    return r.results[0]["yT"].T.reshape(1, T, D)
```

```python
from contextlib import ExitStack

import concourse.bass as bass
from concourse import mybir

ALU = mybir.AluOpType
ACT = mybir.ActivationFunctionType
AX = mybir.AxisListType
F32 = mybir.dt.float32
F32R = mybir.dt.float32r
BF16 = mybir.dt.bfloat16
I8 = mybir.dt.int8

P = 128
D = 1024
T = 1024
KT = D // P
HALF = 512
NH = 4
NC = T // P
HD = 64
AH, KVH = 8, 2
GRP = AH // KVH
VW = (NH * P + KVH * HD) // 2
F = 2816
FT = F // P
EPS = 1e-6
TINY = 1e-18
NEG = -1e30
LEVELS = 7
KB = 1024
N_PROJ = 5 + 3 * NH
N_UNITS = N_PROJ + 9
V_FIRST = 5
W_GAP = 3
LAG = 3
H0_EXTRA = 8
OC_EXTRA = 4
OUT_EARLY = 16
TAIL = 2


def schedule():

    def proj(tiles):
        return [("P", 2 * u + half, part) for u in tiles for half in range(2) for part in range(4)]

    def tile(hd, j):
        return 5 + 3 * hd + j

    def out(group):
        parts = (2, 2, 1)[group]
        return [("O", 16 * group + g, part) for g in range(16) for part in range(parts)]

    def weights_after(d):
        if d[0] == "P" and d[1] % 2 == 1 and d[2] == 3:
            return d[1] // 2 + 2
        if d[0] == "O" and d[1] < 32 and d[1] % 4 == 3 and d[2] == 1:
            return N_PROJ + d[1] // 4 + 2
        return N_UNITS

    due = []

    def mix(dense, steps, lead=0):
        res, k, n = [], 0, len(dense) - lead
        for seen, d in enumerate(dense, 1):
            res.append(d)
            res += [step for left, step in due if left == 1]
            due[:] = [(left - 1, step) for left, step in due if left > 1]
            if weights_after(d) < N_UNITS:
                due.extend([(1, ("W", weights_after(d))), (W_GAP, ("WL", weights_after(d)))])
            while k < len(steps) and seen >= lead and k * n <= (seen - lead) * len(steps):
                res += steps[k]
                k += 1
        for s in steps[k:]:
            res += s
        return res

    dense = [d for hh in range(NH) for j in range(3) for d in proj([tile(hh, j)])]
    dense[-8:] = [("P", 2 * N_PROJ - 2 + half, part) for part in range(4) for half in range(2)]
    n_p = len(dense)
    dense += out(0) + out(1)
    taken = [0]

    def take(n):
        taken[0] += n
        return dense[taken[0] - n:taken[0]]

    order = [("W", 0), ("WL", 0), ("W", 1), ("WL", 1)]
    order += [("V", n, t) for n in range(2) for t in range(NC) if (n, t) > (0, V_FIRST)]
    for u in range(5):
        order += mix(proj([u]), [[("AD", u - 1)], [("AM", u - 1)], [("AN", u - 1)], [("AH", u - 1)], [("AL", u - 1)]]
                     if u else [], lead=2)
        order += [("AS", u)]
    order += mix(take(6), [[("AD", 4)], [("AM", 4)], [("AN", 4)], [("AH", 4)], [("AL", 4)]], lead=1)
    units = 2 * NC
    steps = []
    for i in range(units + LAG + 1):
        steps.append([s for s in (("PV", i - LAG - 1), ("TR", i - LAG), ("SN", i - 2), ("SC", i), ("SE", i - 1))
                      if 0 <= s[1] < units])
    order += mix(take(14), steps[:units]) + mix(take(4), steps[units:units + LAG])
    order += [("H1", 0)]
    steps = [steps[units + LAG], [("HK", 0)], [("HQ", 0)], [("HS", 0)], [("H2", 0)], [("LV", 0, 0)],
             [("HD", 0)], [("LX", 0, 0), ("KT", 0)], [("KE", 0), ("LV", 0, 1), ("LV", 0, 2)]]
    order += mix(take(8 + H0_EXTRA), steps)
    for h in range(NH):
        last = h == NH - 1
        steps = []
        for lv in range(LEVELS):
            steps.append([("LM", h, lv)])
            steps[lv] += [("LX", h, lv + 2)] if lv + 2 < LEVELS else []
            steps[lv] += [("LV", h, lv + 4)] if lv + 4 < LEVELS else []
        steps[0] = [("LX", h, 1), ("LV", h, 3)] + steps[0]
        if h:
            steps[0] += [("OM", h - 1)]
            steps[1] = [("ON", h - 1)] + steps[1]
            steps[2] += [("OX", h - 1, 0)]
            steps[4] += [("OX", h - 1, 1)]
        if last:
            steps[5] += [("FD", 1), ("FD", 0), ("MS", 6), ("ML", 6)]
            order += mix(take(n_p + 32 - taken[0]), steps)
            order += [("FD", 2), ("FD", 3), ("F", 0)]
            steps = [[("OC", h, c)] for c in range(NC)] + [[("OS", h)], [("OM", h)], [("ON", h), ("OX", h, 0), ("OX", h, 1)], [("MS", 7), ("ML", 7)]]
            steps[2] += [("F", 1)]
            steps[5] += [("F", 2)]
            order += mix(take(len(dense) - taken[0]), steps)
        else:
            if h == NH - 2:
                for step in mix(take(n_p - taken[0]), steps[:6]):
                    order += [step]
                    if step[:2] == ("P", 2 * N_PROJ - 1):
                        order += [("MS", step[2])] + ([("ML", step[2] - 1)] if step[2] else [])
                order += [("ML", 3)] + mix(take(TAIL), steps[6:])
            else:
                order += mix(take(24 * (h + 2) - taken[0]), steps)
            order += [step for _, step in due if step[0] == "W"] + [("H1", h + 1)]
            due[:] = [(left, step) for left, step in due if step[0] != "W"]
            steps = [[("OC", h, c)] for c in range(NC)] + [[("OS", h)]]
            steps[1] += [("HK", h + 1)]
            steps[2] += [("HQ", h + 1)]
            steps[3] += [("HS", h + 1)]
            steps[4] += [("H2", h + 1)]
            steps[5] += [("LV", h + 1, 0)]
            steps[6] += [("HD", h + 1)]
            steps[8] += [("LX", h + 1, 0), ("KT", h + 1)]
            steps += [[("KE", h + 1), ("LV", h + 1, 1), ("LV", h + 1, 2)]]
            if h == NH - 2:
                steps[5] += [("MS", 4)]
                steps[6] += [("ML", 4), ("MS", 5)]
                steps[7] += [("ML", 5)]
                order += mix(take(OUT_EARLY - TAIL), steps)
            else:
                order += mix(take(8 + OC_EXTRA), steps, lead=1)
    order += [("FD", 4), ("FD", 5)] + [("O", 32, 0), ("O", 33, 0), ("NL", 0), ("O", 34, 0), ("O", 35, 0)]
    for m in range(KT):
        order += ([("NL", m + 1)] if m < KT - 1 else []) + [("N2", m)]
        order += [("O", 36 + 2 * m + half, 0) for half in range(2) if m < KT - 2]
    order += [("F", 3), ("F", 4), ("F", 5)]
    return order


def build(nc, xT, wv, wproj, wo_a, wo_b, wo_c, wg, wu, wd, gain1, gain2, lbl, ogain, qgain, kgain, sinks, yT):
    ctx = ExitStack()
    with ctx:
        used = {}

        def at(name, kb, shape, dt=F32):
            return nc.alloc_sbuf_tensor_at(name, shape, dt, offset=16640 + int(kb * KB))

        def sem(name):
            return ctx.enter_context(nc.semaphore(name))

        ones = at("ones", 0, [P, P])
        ident = at("ident", 0.5, [P, P])
        blk = at("blk", 1, [P, P])
        blkr = at("blkr", 1, [P, P], F32R)
        wmask = at("wmask", 1.5, [P, 2 * P])
        lmask = at("lmask", 2.5, [P, LEVELS, P], I8)
        scan_keep = at("scan_keep", 3.5, [P, T], BF16)
        S = at("S", 5.5, [P, 2, P])
        small = at("small", 6.5, [P, 120])
        g1, g2 = small[:, 0:8], small[:, 8:16]
        lb_in = small[:, 16:24]
        lb_e, lb_m = small[:, 24:32], small[:, 32:36]
        lb, omlb, nomlb = small[:, 36:40], small[:, 40:44], small[:, 44:48]
        og, qg, kg = small[:, 48:49], small[:, 49:50], small[:, 50:51]
        eps = small[:, 51:52]
        sink, nsink = small[:, 52:60], small[:, 60:68]
        ebt = small[:, 68:84]
        lb_s = small[:, 84:88]
        rtok = small[:, 88:96]
        smax = at("smax", 207, [P, 60])
        nmax, rsum, esink, den, rden = (smax[:, 12 * i:12 * i + 12] for i in range(5))
        uhi = at("uhi", 7, [P, KT, T], F32R)
        ulo = at("ulo", 39, [P, KT, T], F32R)
        h = at("h", 7, [P, KT, T])
        mhi0 = at("mhi0", 39, [P, 4, T], F32R)
        mlo0 = at("mlo0", 55, [P, 4, T], F32R)
        v = at("v", 71, [P, NC, 2 * VW])
        sq = at("sq", 71, [P, 4, T])
        mhi3 = at("mhi3", 71, [P, T], F32R)
        mlo3 = at("mlo3", 75, [P, T], F32R)
        x = at("x", 91, [P, KT, T])
        att = at("att", 91, [P, 4, T])
        rec = at("rec", 107, [P, NH, T])
        mhi1 = at("mhi1", 91, [P, 4, T], F32R)
        mlo1 = at("mlo1", 107, [P, NH, T], F32R)
        wraw = [at(f"wraw{i}", 123 + 4 * i, [P, KT * P]) for i in range(2)]
        whi = [at(f"whi{i}", 131 + 4 * i, [P, KT * P], F32R) for i in range(2)]
        wlo = [at(f"wlo{i}", 139 + 4 * i, [P, KT * P], F32R) for i in range(2)]
        vraw = at("vraw", 147, [P, KT * VW])
        vhi = [at(f"vhi{i}", 157 + 10 * i, [P, KT * VW], F32R) for i in range(2)]
        vlo = [at(f"vlo{i}", 177 + 10 * i, [P, KT * VW], F32R) for i in range(2)]
        kq = at("kq", 147, [P, 5, T])
        kqhi = at("kqhi", 147, [P, 5, T], F32R)
        kqn = [at(f"kqn{i}", kb, [P, T]) for i, kb in enumerate((199, 107, 111, 115, 119))]
        kqlo = [at(f"kqlo{i}", kb, [P, T], F32R) for i, kb in enumerate((199, 107, 111, 115, 119))]
        sc = at("sc", 167, [P, 3, GRP, 2 * P])
        asq = at("asq", 167, [P, 2, T])
        asqhi, asqlo = at("asqhi", 175, [P, T], F32R), at("asqlo", 179, [P, T], F32R)
        pT = at("pT", 179, [P, 2, GRP * P])
        ars = at("ars", 183, [P, T])
        K = at("K", 147, [P, T])
        Q = at("Q", 151, [P, T])
        B = at("B", 155, [P, T])
        DD = [at("D0", 159, [P, T]), at("D1", 163, [P, T])]
        M = [at("M0", 167, [P, T]), at("M1", 171, [P, T])]
        A = at("A", 175, [P, T])
        X0 = at("X0", 179, [P, T])
        KDT = at("KDT", 183, [P, NC, P])
        rawf, rawq = at("rawf", 187, [P, T]), at("rawq", 191, [P, T])
        rawg = [at("rawg0", 195, [P, T]), at("rawg1", 199, [P, T])]
        rs = at("rs", 203, [P, T])

        def qi(hh):
            return rec[:, hh + 1, :] if hh < NH - 1 else X0[:, :]

        def on_tmp(hh):
            return (X0, X0, rawf, M[0])[hh]

        u2hi = at("u2hi", 39, [P, KT, T], F32R)
        u2lo = at("u2lo", 91, [P, KT, T], F32R)
        nsq = at("nsq", 79, [P, 2, T])
        nacc = at("nacc", 87, [P, T])
        nrs = at("nrs", 131, [P, T])
        hidhi = at("hidhi", 71, [P, 2, T], F32R)
        hidlo = at("hidlo", 79, [P, 2, T], F32R)
        gate = [at("gate01", 87, [P, 2, HALF]), at("gate23", 123, [P, 2, HALF])]
        hid = at("hid", 127, [P, 2, HALF])
        fraw = [at(f"fraw{p}", kb, [P, KT * P]) for p, kb in enumerate((187, 191, 155, 171, 179, 167))]
        fhi = [at(f"fhi{p}", kb, [P, KT * P], F32R) for p, kb in enumerate((195, 147, 159, 175, 199, 139))]
        flo = [at(f"flo{p}", kb, [P, KT * P], F32R) for p, kb in enumerate((203, 151, 163, 183, 135, 143))]

        ps = ctx.enter_context(nc.psum_tensor("ps", [P, 8, HALF], F32))

        s_const, s_g1 = sem("consts_in"), sem("gain1_in")
        s_x = [sem(f"x_in{k}") for k in range(KT)]
        s_vraw = [sem(f"vraw_in{i}") for i in range(KT)]
        s_vhi, s_vlo = sem("v_weights_hi"), sem("v_weights_lo")
        s_wraw = [sem("wraw0_in"), sem("wraw1_in")]
        s_whi, s_wlo = sem("unit_hi"), sem("unit_lo")
        s_pool0, s_setup = sem("pool_setup_step"), sem("setup_done")
        s_lb = sem("lb_step")
        s_lbact = sem("lb_exp")
        s_sq, s_acc, s_ss, s_ln, s_rs = (sem("n1_square"), sem("n1_added"), sem("n1_sum"), sem("n1_ln"),
                                         sem("n1_rstd"))
        s_uhi, s_ulo = sem("u_hi"), sem("u_lo")
        s_rt, s_rtok = sem("rstd_t"), sem("rstd_by_token")
        s_vmm, s_vev = sem("value_group"), sem("value_evac")
        s_pmm, s_pev, s_ufree = sem("proj_group"), sem("proj_evac"), sem("u_tiles_free")
        s_blk, s_ash, s_asl = sem("blk_ready"), sem("an_sq_hi"), sem("an_sq_lo")
        s_asq, s_ass, s_aln, s_ars, s_an = sem("an_sq"), sem("an_sum"), sem("an_ln"), sem("an_rstd"), sem("an_done")
        s_kqhi, s_kqlo = sem("kq_hi"), sem("kq_lo")
        s_scm, s_masked, s_amx, s_anm, s_asn = (sem("scores"), sem("scores_masked"), sem("row_max"),
                                                sem("row_nmax"), sem("sink_arg"))
        s_exp, s_den, s_rden, s_prob = sem("att_exp"), sem("att_den"), sem("att_rden"), sem("probs")
        s_tr, s_pte0, s_pte1 = sem("probs_t"), sem("probs_t_prev_evac"), sem("probs_t_cur_evac")
        s_pv, s_attev = sem("att_out"), sem("att_out_evac")
        s_sig, s_kq, s_lnf, s_scan, s_gm = sem("sigmoids"), sem("k_and_q"), sem("log_f"), sem("decay_sums"), sem("swish_g")
        s_eb, s_qi, s_d2, s_e2, s_kd = sem("exp_b"), sem("qi"), sem("tail_sum"), sem("exp_tail"), sem("kd")
        s_kt, s_kte = sem("kd_t"), sem("kd_t_evac")
        s_lvs, s_lve, s_lvm, s_lmm, s_cp = sem("lv_sub"), sem("lv_exp"), sem("lv_mul"), sem("lv_product"), sem("lv_kept")
        s_kv, s_oc, s_st, s_oev = sem("state_product"), sem("chunk_output"), sem("state"), sem("o_evac")
        s_osq, s_oss, s_oln, s_ors, s_on1, s_on = (sem("o_square"), sem("o_sum"), sem("o_ln"), sem("o_rstd"),
                                                   sem("o_normed"), sem("o_done"))
        s_mhi, s_mlo = sem("mix_hi"), sem("mix_lo")
        s_omm, s_oadd = sem("out_group"), sem("out_added")
        s_nsq, s_nacc, s_nss, s_nln, s_nrs = (sem("n2_square"), sem("n2_added"), sem("n2_sum"), sem("n2_ln"),
                                              sem("n2_rstd"))
        s_u2hi, s_u2lo = sem("u2_hi"), sem("u2_lo")
        s_fraw = [sem(f"fraw{p}_in") for p in range(6)]
        s_fhi, s_flo = sem("ffn_w_hi"), sem("ffn_w_lo")
        s_gsc, s_gr = sem("gate_scaled"), sem("silu_scaled")
        s_fmm, s_silu, s_hid, s_hhi, s_hlo = (sem("gate_up_group"), sem("gate_silu"), sem("hidden"),
                                              sem("hidden_hi"), sem("hidden_lo"))
        s_dmm, s_dadd = sem("down_group"), sem("down_added")
        s_out = sem("y_out")

        order = schedule()
        N_CONST = 6

        def nk(i):
            return P if i < 2 else 2 * P

        def tr_count(i):
            return i + 1 if i < 2 else 2 * i

        def first_in_halves(m):
            return ((1, slice(0, HALF)), (2, slice(HALF, T))) if m == 0 else ((2, slice(0, T)),)

        def unit_used(u):
            return (s_pmm, 2 * (u + 1)) if u < N_PROJ else (s_omm, 4 * (u - N_PROJ + 1))

        def out_bank(g):
            return (2 * N_PROJ + g) % 3 if g < 32 else (0, 1, 2, 7)[g % 4]

        def down_bank(first, g):
            return ((3, 4, 5, 6), (0, 1, 2, 7))[g // 4 % 2][g % 4] if first else g % 8

        def ffn_bank(first, p, half):
            return ((3, 4), (5, 6), (0, 1), (2, 7))[p][half] if first else 2 * p + half

        block = ctx.enter_context(nc.Block())

        @block.sync
        def _(sp):
            xv = xT.rearrange("(k p) t -> k p t", p=P)
            sp.dma_start(g1, gain1).then_inc(s_g1, 16)
            for k in range(KT):
                sp.dma_start(vraw[:, k * VW:(k + 1) * VW], wv[0, :, k * VW:(k + 1) * VW]).then_inc(s_vraw[k], 16)
                sp.dma_start(x[:, k, :], xv[k, :, :]).then_inc(s_x[k], 16)
            for dst, src in ((g2, gain2), (lb_in, lbl), (og, ogain), (sink, sinks), (qg, qgain), (kg, kgain)):
                sp.dma_start(dst, src).then_inc(s_const, 16)
            for step in order:
                if step[0] == "W":
                    u = step[1]
                    if u >= 2:
                        sp.wait_ge(s_wlo, u - 1)
                    if u < N_PROJ:
                        src = wproj[u, :, :]
                    elif u < N_PROJ + 4:
                        src = wo_a[u - N_PROJ, :, :]
                    elif u < N_PROJ + 8:
                        src = wo_b[u - N_PROJ - 4, :, :]
                    else:
                        src = wo_c
                    sp.dma_start(wraw[u % 2][:, 0:src.shape[1]], src).then_inc(s_wraw[u % 2], 16)
                if step == ("W", 1):
                    for i in range(KT):
                        sp.wait_ge(s_vlo, i + 1)
                        sp.dma_start(vraw[:, i * VW:(i + 1) * VW], wv[1, :, i * VW:(i + 1) * VW])\
                            .then_inc(s_vraw[i], 16)
                if step[0] == "MS" and step[1] < 3 or step == ("W", N_PROJ + 1):
                    i = step[1] if step[1] < 3 else 3
                    sp.wait_ge(*((s_ufree, i + 1) if i < 3 else (s_pmm, 2 * N_PROJ)))
                    for k in (i,) if i < 3 else range(3, KT):
                        sp.dma_start(h[:, k, :], xv[k, :, :]).then_inc(s_x[k], 16)
                if step[0] == "FD":
                    p = step[1]
                    sp.wait_ge(*((s_on, 3), (s_kq, 8), (s_lmm, 2 * LEVELS * NH), (s_lmm, 2 * LEVELS * NH), (s_oc, 32), (s_on, 4))[p])
                    sp.dma_start(fraw[p][:, :], (wg[0], wu[0], wg[1], wu[1], wd[0], wd[1])[p]).then_inc(s_fraw[p], 16)
            with sp.Fori(0, FT // 2 - 1) as i:
                for p in range(6):
                    sp.wait_ge(s_flo, 6 * i + (p + 1))
                    w = (wg, wu, wg, wu, wd, wd)[p]
                    j = (0, 0, 1, 1, 0, 1)[p]
                    sp.dma_start(fraw[p][:, :], w[bass.ds(2 * i + (2 + j), 1), :, :].rearrange("a p n -> (a p) n"))\
                        .then_inc(s_fraw[p], 16)
            yv = yT.rearrange("(k p) t -> k p t", p=P)
            for m in range(KT):
                sp.wait_ge(s_dadd, 16 * (FT // 2 - 1) + 2 * m + 2)
                sp.dma_start(yv[m, :, :], h[:, m, :]).then_inc(s_out, 16)
            sp.wait_ge(s_out, 16 * KT)

        @block.gpsimd
        def _(pool):
            n0 = [0]

            def step0(ins):
                n0[0] += 1
                ins.then_inc(s_pool0, 1)
                pool.wait_ge(s_pool0, n0[0])

            step0(nc.gpsimd.memset(ones[:, :], 1.0))
            step0(nc.gpsimd.memset(eps, EPS))
            step0(nc.gpsimd.memset(ident[:, :], 0.0))
            step0(nc.gpsimd.affine_select(out=ident[:, :], in_=ident[:, :], compare_op=ALU.not_equal, fill=1.0,
                                          base=0, pattern=[[-1, P]], channel_multiplier=1))
            for k in range(1, KT):
                pool.wait_ge(s_sq, k + 1)
                if k > 1:
                    pool.wait_ge(s_acc, k - 1)
                nc.gpsimd.tensor_tensor(sq[:, 0, :], sq[:, 0, :], sq[:, 1 + k % 3, :], ALU.add).then_inc(s_acc, 1)
            step0(nc.gpsimd.memset(blk[:, :], 0.0))
            step0(nc.gpsimd.memset(blk[0:HD, 0:HD], 1.0))
            step0(nc.gpsimd.memset(blk[HD:P, HD:P], 1.0))
            step0(nc.gpsimd.memset(wmask[:, :], 0.0))
            step0(nc.gpsimd.affine_select(out=wmask[:, :], in_=wmask[:, :], compare_op=ALU.is_gt, fill=NEG,
                                          base=0, pattern=[[1, 2 * P]], channel_multiplier=-1))
            step0(nc.gpsimd.affine_select(out=wmask[:, :], in_=wmask[:, :], compare_op=ALU.is_ge, fill=NEG,
                                          base=P, pattern=[[-1, 2 * P]], channel_multiplier=1))
            step0(nc.gpsimd.memset(lmask[:, :, :], 0.0))
            for lv in range(LEVELS):
                L = 1 << lv
                up = lmask[:, lv, :].rearrange("p (b u l) -> p b u l", u=2, l=L)[:, :, 1, :]
                nb = P // (2 * L)
                step0(nc.gpsimd.memset(up, 1.0))
                step0(nc.gpsimd.affine_select(out=up, in_=up, compare_op=ALU.is_ge, fill=0.0, base=0,
                                              pattern=[[-2 * L, nb], [0, L]], channel_multiplier=1))
                step0(nc.gpsimd.affine_select(out=up, in_=up, compare_op=ALU.is_ge, fill=0.0, base=L - 1,
                                              pattern=[[2 * L, nb], [0, L]], channel_multiplier=-1))
            step0(nc.gpsimd.affine_select(out=lmask[:, 0, :], in_=lmask[:, 0, :],
                                          compare_op=ALU.not_equal, fill=1.0, base=0, pattern=[[-1, P]],
                                          channel_multiplier=1))
            step0(nc.gpsimd.memset(scan_keep[:, :], 1.0))
            nc.gpsimd.memset(scan_keep[:, 0:T:P], 0.0).then_inc(s_setup, 1)
            for step in order:
                if step[0] == "AS":
                    i = step[1]
                    pool.wait_ge(s_pev, 2 * i + 2)
                    if i >= 2:
                        pool.wait_ge(s_asl, i - 1)
                    nc.gpsimd.tensor_tensor(asq[:, i % 2, :], kq[:, i, :], kq[:, i, :], ALU.mult).then_inc(s_asq, 1)
                elif step[0] == "SN":
                    i = step[1]
                    r, n_keys = i % 3, nk(i)
                    pool.wait_ge(s_rden, i + 1)
                    probs = sc[:, r, :, 0:n_keys]
                    nc.gpsimd.tensor_tensor(probs, probs, rden[:, 4 * r:4 * r + 4].unsqueeze(2)
                                            .broadcast_to([P, GRP, n_keys]), ALU.mult).then_inc(s_prob, 1)
                elif step[0] == "H1":
                    hh = step[1]
                    if hh == 0:
                        pool.wait_ge(s_tr, tr_count(2 * NC - 1))
                        nc.gpsimd.memset(A[:, :], 0.0).then_inc(s_setup, 1)
                    pool.wait_ge(s_sig, 3 * hh + 3)
                    gv = rawg[hh % 2]
                    nc.gpsimd.tensor_tensor(gv[:, :], gv[:, :], DD[0][:, :], ALU.mult).then_inc(s_gm, 1)
                elif step[0] == "H2":
                    hh = step[1]
                    pool.wait_ge(s_eb, 2 * hh + 1)
                    pool.wait_ge(s_kq, 2 * hh + 2)
                    if hh == NH - 1:
                        pool.wait_ge(s_on, 2)
                    nc.gpsimd.tensor_tensor(qi(hh), Q[:, :], DD[0][:, :], ALU.mult).then_inc(s_qi, 1)
                elif step[0] == "LV":
                    _, hh, lv = step
                    L = 1 << lv
                    if lv == 0:
                        pool.wait_ge(s_qi, hh + 1)
                    elif lv == 1:
                        pool.wait_ge(s_kt, 2 * hh + 2)
                    else:
                        pool.wait_ge(s_lvm, 2 * (7 * hh + lv - 1))
                    b4 = B[:, :].rearrange("p (b l) -> p b l", l=2 * L)
                    mid = b4[:, :, L - 1:L].broadcast_to([P, T // (2 * L), 2 * L])
                    nc.gpsimd.tensor_tensor(DD[lv % 2][:, :].rearrange("p (b l) -> p b l", l=2 * L), b4, mid,
                                            ALU.subtract).then_inc(s_lvs, 1)
            for m in range(1, KT):
                pool.wait_ge(s_nsq, m + 1)
                if m > 1:
                    pool.wait_ge(s_nacc, m - 1)
                nc.gpsimd.tensor_tensor(nacc[:, :], nacc[:, :], nsq[:, m % 2, :], ALU.add).then_inc(s_nacc, 1)
            pool.wait_ge(s_nrs, 1)
            with pool.Fori(0, FT // 2) as i:
                for j in range(2):
                    for half in range(2):
                        pool.wait_ge(s_silu, 4 * i + (2 * j + half + 1))
                        gv = gate[j][:, half, :]
                        nc.gpsimd.tensor_tensor(gv, gv, nrs[:, half * HALF:(half + 1) * HALF], ALU.mult)\
                            .then_inc(s_gr, 1)

        @block.scalar
        def _(act):
            nc.scalar.preload_act_table_set("natural_log_exp_and_others")
            act.wait_ge(s_g1, 16)
            for k in range(KT):
                act.wait_ge(s_vraw[k], 16)
                nc.scalar.activation(vhi[0][:, k * VW:(k + 1) * VW], vraw[:, k * VW:(k + 1) * VW], ACT.Copy)\
                    .then_inc(s_vhi, 1)
                act.wait_ge(s_x[k], 16)
                nc.scalar.activation(uhi[:, k, :], x[:, k, :], ACT.Copy, scale=g1[:, k:k + 1]).then_inc(s_uhi, 1)
                if k >= 4:
                    act.wait_ge(s_acc, k - 3)
                nc.scalar.activation(sq[:, 1 + k % 3 if k else 0, :], x[:, k, :], ACT.Square).then_inc(s_sq, 1)
            act.wait_ge(s_pool0, 2)
            act.wait_ge(s_ss, 2)
            nc.scalar.activation(rs[:, :], ps[:, 6:8, :], ACT.Ln, scale=1.0 / D, bias=eps).then_inc(s_ln, 1)
            act.wait_ge(s_ln, 1)
            nc.scalar.activation(rs[:, :], rs[:, :], ACT.Exp, scale=-0.5).then_inc(s_rs, 1)
            for i in range(KT):
                act.wait_ge(s_vraw[i], 32)
                nc.scalar.activation(vhi[1][:, i * VW:(i + 1) * VW], vraw[:, i * VW:(i + 1) * VW], ACT.Copy)\
                    .then_inc(s_vhi, 1)
            act.wait_ge(s_rt, 1)
            nc.scalar.activation(rtok, ps[:, 6:8, :].rearrange("p b (t c) -> p (b t) c", c=P)[:, :, 0], ACT.Copy)\
                .then_inc(s_rtok, 1)
            act.wait_ge(s_rtok, 1)

            def value_out(g):
                n, t = g // NC, g % NC
                act.wait_ge(s_vmm, g + 1)
                nc.scalar.activation(v[:, t, n * VW:(n + 1) * VW], ps[:, g % 8, 0:VW], ACT.Copy,
                                     scale=rtok[:, t:t + 1]).then_inc(s_vev, 1)

            for g in range(V_FIRST + 1):
                value_out(g)
            for step in order:
                kind = step[0]
                if kind == "W":
                    u = step[1]
                    act.wait_ge(s_wraw[u % 2], 16 * (u // 2 + 1))
                    if u >= 2:
                        act.wait_ge(*unit_used(u - 2))
                    n = 6 * P if N_PROJ + 4 <= u < N_PROJ + 8 else 8 * P
                    nc.scalar.activation(whi[u % 2][:, 0:n], wraw[u % 2][:, 0:n], ACT.Copy).then_inc(s_whi, 1)
                    if u == 1:
                        act.wait_ge(s_lb, 2)
                        nc.scalar.activation(lb_e, lb_e, ACT.Exp).then_inc(s_lbact, 1)
                elif kind == "V":
                    value_out(step[1] * NC + step[2])
                elif kind == "AS":
                    i = step[1]
                    if i == 0:
                        act.wait_ge(s_setup, 1)
                        nc.scalar.activation(blkr[:, :], blk[:, :], ACT.Copy).then_inc(s_blk, 1)
                    act.wait_ge(s_pev, 2 * i + 2)
                    if i:
                        act.wait_ge(s_ass, 2 * i)
                    nc.scalar.activation(asqhi[:, :], kq[:, i, :], ACT.Square).then_inc(s_ash, 1)
                elif kind == "AN":
                    i = step[1]
                    act.wait_ge(s_ass, 2 * i + 2)
                    if i:
                        act.wait_ge(s_an, i)
                    nc.scalar.activation(ars[:, :], ps[:, 3:5, :], ACT.Ln, scale=1.0 / HD, bias=eps)\
                        .then_inc(s_aln, 1)
                    act.wait_ge(s_aln, i + 1)
                    nc.scalar.activation(ars[:, :], ars[:, :], ACT.Exp, scale=-0.5).then_inc(s_ars, 1)
                elif kind == "AH":
                    i = step[1]
                    act.wait_ge(s_an, i + 1)
                    nc.scalar.activation(kqhi[:, i, :], kqn[i][:, :], ACT.Copy).then_inc(s_kqhi, 1)
                elif kind == "SE":
                    i = step[1]
                    r, n_keys = i % 3, nk(i)
                    act.wait_ge(s_anm, i + 1)
                    for j in range(GRP):
                        nc.scalar.activation(sc[:, r, j, 0:n_keys], sc[:, r, j, 0:n_keys], ACT.Exp,
                                             bias=nmax[:, 4 * r + j:4 * r + j + 1],
                                             accum_out=rsum[:, 4 * r + j:4 * r + j + 1]).then_inc(s_exp, 1)
                    act.wait_ge(s_asn, i + 1)
                    nc.scalar.activation(esink[:, 4 * r:4 * r + 4], esink[:, 4 * r:4 * r + 4], ACT.Exp)\
                        .then_inc(s_exp, 1)
                elif kind == "TR":
                    i = step[1]
                    if i >= 2:
                        act.wait_ge(s_tr, tr_count(i) - 1)
                        act.wait_ge(s_pv, i)
                        nc.scalar.activation(pT[:, 0, :], ps[:, 5, :], ACT.Copy).then_inc(s_pte0, 1)
                elif kind == "PV":
                    i = step[1]
                    if i % 2 == 1:
                        n = i // 2
                        act.wait_ge(s_pv, i + 1)
                        nc.scalar.activation(att[:, :, n * P:(n + 1) * P],
                                             ps[:, 7, :].rearrange("p (i q) -> p i q", q=P), ACT.Copy)\
                            .then_inc(s_attev, 1)
                elif kind == "H1":
                    hh = step[1]
                    act.wait_ge(s_pev, 2 * (5 + 3 * hh + 3))
                    if hh == 0:
                        act.wait_ge(s_scm, 2 * NC)
                    else:
                        act.wait_ge(s_lvm, 14 * hh)
                    nc.scalar.activation(rawf[:, :], rawf[:, :], ACT.Sigmoid).then_inc(s_sig, 1)
                    nc.scalar.activation(DD[1][:, :], rawq[:, :], ACT.Sigmoid).then_inc(s_sig, 1)
                    nc.scalar.activation(DD[0][:, :], rawg[hh % 2][:, :], ACT.Sigmoid).then_inc(s_sig, 1)
                    nc.scalar.preload_act_table_set("natural_log_exp_and_others")
                    act.wait_ge(s_sig, 3 * hh + 1)
                    nc.scalar.activation(B[:, :], rawf[:, :], ACT.Ln, scale=omlb[:, hh:hh + 1],
                                         bias=lb[:, hh:hh + 1]).then_inc(s_lnf, 1)
                elif kind == "H2":
                    hh = step[1]
                    act.wait_ge(s_scan, hh + 1)
                    act.wait_ge(s_gm, hh + 1)
                    nc.scalar.activation(DD[0][:, :], B[:, :], ACT.Exp).then_inc(s_eb, 1)
                    if hh >= 2:
                        act.wait_ge(s_st, NC * (hh - 1))
                    nc.scalar.activation(ebt[:, 8 * (hh % 2):8 * (hh % 2) + 8], B[:, P - 1:T:P], ACT.Exp)\
                        .then_inc(s_eb, 1)
                    act.wait_ge(s_d2, hh + 1)
                    nc.scalar.activation(DD[1][:, :], DD[1][:, :], ACT.Exp).then_inc(s_e2, 1)
                elif kind == "KE":
                    hh = step[1]
                    for x2 in range(2):
                        act.wait_ge(s_kt, 2 * hh + x2 + 1)
                        if hh and not x2:
                            act.wait_ge(s_oc, NC * hh)
                        nc.scalar.activation(KDT[:, 4 * x2:4 * x2 + 4, :], ps[:, 3 + x2, :], ACT.Copy)\
                            .then_inc(s_kte, 1)
                elif kind == "LV":
                    _, hh, lv = step
                    L = 1 << lv
                    act.wait_ge(s_lvs, 7 * hh + lv + 1)
                    if lv == 0:
                        act.wait_ge(*((s_lmm, 14 * hh) if hh else (s_tr, tr_count(2 * NC - 1))))
                        nc.scalar.activation(M[1][:, :], DD[0][:, :], ACT.Exp, scale=-1.0).then_inc(s_lve, 1)
                        act.wait_ge(s_lve, 14 * hh + 1)
                        nc.scalar.activation(DD[0][:, :], DD[0][:, :], ACT.Exp).then_inc(s_lve, 1)
                        continue
                    dv = DD[lv % 2][:, :].rearrange("p (b u l) -> p b u l", u=2, l=L)
                    nc.scalar.activation(dv[:, :, 0, :], dv[:, :, 0, :], ACT.Exp, scale=-1.0).then_inc(s_lve, 1)
                    nc.scalar.activation(dv[:, :, 1, :], dv[:, :, 1, :], ACT.Exp).then_inc(s_lve, 1)
                elif kind == "OC":
                    _, hh, c = step
                    if c % 4 == 3:
                        x2 = c // 4
                        act.wait_ge(s_oc, NC * hh + c + 1)
                        nc.scalar.activation(rec[:, hh, x2 * HALF:(x2 + 1) * HALF], ps[:, 5 + x2, :], ACT.Copy)\
                            .then_inc(s_oev, 1)
                elif kind == "OS":
                    hh = step[1]
                    act.wait_ge(s_oev, 2 * hh + 2)
                    if hh:
                        act.wait_ge(*((s_on1, hh), (s_kq, 2 * NH - 1), (s_lmm, 2 * LEVELS * NH))[hh - 1])
                    nc.scalar.activation(on_tmp(hh)[:, :], rec[:, hh, :], ACT.Square).then_inc(s_osq, 1)
                elif kind == "ON":
                    hh = step[1]
                    act.wait_ge(s_oss, 2 * hh + 2)
                    nc.scalar.activation(on_tmp(hh)[:, :], ps[:, 5:7, :], ACT.Ln, scale=1.0 / P, bias=eps)\
                        .then_inc(s_oln, 1)
                    act.wait_ge(s_oln, hh + 1)
                    nc.scalar.activation(on_tmp(hh)[:, :], on_tmp(hh)[:, :], ACT.Exp, scale=-0.5).then_inc(s_ors, 1)
                elif kind == "MS":
                    i = step[1]
                    if i < 4:
                        act.wait_ge(*((s_ufree, i + 1) if i < 3 else (s_pmm, 2 * N_PROJ)))
                        dst, src = mhi0[:, i, :], att[:, i, :]
                    else:
                        act.wait_ge(s_on, i - 3)
                        act.wait_ge(s_mlo, 4)
                        src = rec[:, i - 4, :]
                        dst = mhi1[:, i - 4, :] if i < 7 else mhi3[:, :]
                    nc.scalar.activation(dst, src, ACT.Copy).then_inc(s_mhi, 1)
                elif kind == "NL":
                    m = step[1]
                    for x2, cols in first_in_halves(m):
                        act.wait_ge(s_oadd, 32 + 2 * m + x2)
                        nc.scalar.activation(u2hi[:, m, cols], h[:, m, cols], ACT.Copy, scale=g2[:, m:m + 1])\
                            .then_inc(s_u2hi, 1)
                    if m >= 3:
                        act.wait_ge(s_nacc, m - 2)
                    dst = nsq[:, m % 2, :] if m else nacc[:, :]
                    nc.scalar.activation(dst, h[:, m, :], ACT.Square).then_inc(s_nsq, 1)
                elif kind == "F":
                    p = step[1]
                    act.wait_ge(s_fraw[p], 16)
                    act.wait_ge(*((s_on, 3), (s_lmm, 2 * LEVELS * NH), (s_lmm, 2 * LEVELS * NH), (s_oc, 32), (s_on, 4), (s_omm, 48))[p])
                    nc.scalar.activation(fhi[p][:, :], fraw[p][:, :], ACT.Copy).then_inc(s_fhi, 1)

            act.wait_ge(s_nss, 2)
            nc.scalar.activation(nrs[:, 0:HALF], ps[:, 2, :], ACT.Ln, scale=1.0 / D, bias=eps).then_inc(s_nln, 1)
            nc.scalar.activation(nrs[:, HALF:T], ps[:, 7, :], ACT.Ln, scale=1.0 / D, bias=eps).then_inc(s_nln, 1)
            act.wait_ge(s_nln, 2)
            nc.scalar.activation(nrs[:, :], nrs[:, :], ACT.Exp, scale=-0.5).then_inc(s_nrs, 1)

            def ffn(i, last):
                for j in range(2):
                    for half in range(2):
                        act.wait_ge(s_gsc, 4 * i + (2 * j + half + 1))
                        nc.scalar.activation(gate[j][:, half, :], gate[j][:, half, :], ACT.Silu).then_inc(s_silu, 1)
                    for half in range(2):
                        act.wait_ge(s_hid, 4 * i + (2 * j + half + 1))
                        nc.scalar.activation(hidhi[:, j, half * HALF:(half + 1) * HALF], hid[:, half, :], ACT.Copy)\
                            .then_inc(s_hhi, 1)
                    for p in () if last else (2 * j, 2 * j + 1):
                        act.wait_ge(s_fraw[p], 16 * i + 32)
                        act.wait_ge(s_fmm, 8 * i + (2 * p + 2))
                        nc.scalar.activation(fhi[p][:, :], fraw[p][:, :], ACT.Copy).then_inc(s_fhi, 1)
                for p in () if last else (4, 5):
                    act.wait_ge(s_fraw[p], 16 * i + 32)
                    act.wait_ge(s_dmm, 16 * i + 16)
                    nc.scalar.activation(fhi[p][:, :], fraw[p][:, :], ACT.Copy).then_inc(s_fhi, 1)

            with act.Fori(0, FT // 2 - 1) as i:
                ffn(i, False)
            ffn(FT // 2 - 1, True)

        @block.tensor
        def _(pe):
            def three(out, whi_, wlo_, xhi_, xlo_, first, last):
                nc.tensor.matmul(out, whi_, xhi_, start=first, stop=False)
                nc.tensor.matmul(out, whi_, xlo_, start=False, stop=False)
                return nc.tensor.matmul(out, wlo_, xhi_, start=False, stop=last)

            def value_part(g, k):
                n, t = g // NC, g % NC
                tok, w = slice(t * P, (t + 1) * P), slice(k * VW, (k + 1) * VW)
                return three(ps[:, g % 8, 0:VW], uhi[:, k, tok], ulo[:, k, tok], vhi[n][:, w], vlo[n][:, w],
                             k == 0, k == KT - 1)

            pe.wait_ge(s_pool0, 2)
            for k in range(KT):
                pe.wait_ge(s_vlo, k + 1)
                pe.wait_ge(s_ulo, k + 1)
                for g in range(V_FIRST):
                    mm = value_part(g, k)
                    if k == KT - 1:
                        mm.then_inc(s_vmm, 1)
            pe.wait_ge(s_acc, KT - 1)
            for half in range(2):
                nc.tensor.matmul(ps[:, 6 + half, :], ones[:, :], sq[:, 0, half * HALF:(half + 1) * HALF],
                                 start=True, stop=True).then_inc(s_ss, 1)
            for k in range(KT):
                mm = value_part(V_FIRST, k)
            mm.then_inc(s_vmm, 1)
            pe.wait_ge(s_rs, 1)
            pe.wait_ge(s_pool0, 4)
            for t in range(NC):
                mm = nc.tensor.transpose(ps[:, 6 + t // 4, (t % 4) * P:(t % 4 + 1) * P],
                                         rs[:, t * P:(t + 1) * P], ident[:, :])
            mm.then_inc(s_rt, 1)
            for step in order:
                kind = step[0]
                if kind == "V":
                    _, n, t = step
                    g = n * NC + t
                    if g == V_FIRST + 1:
                        pe.wait_ge(s_rtok, 1)
                    if g >= NC:
                        pe.wait_ge(s_vev, g - 7)
                    for k in range(KT):
                        if g == NC:
                            pe.wait_ge(s_vlo, KT + k + 1)
                        mm = value_part(g, k)
                    mm.then_inc(s_vmm, 1)
                elif kind == "P":
                    _, g, part = step
                    u, half = g // 2, g % 2
                    if part == 0:
                        pe.wait_ge(*((s_vev, NC + g + 1) if g < 3 else (s_pev, g - 2)))
                        pe.wait_ge(s_wlo, u + 1)
                    for k in (part, part + 4) if u == N_PROJ - 1 else (2 * part, 2 * part + 1):
                        w = slice(k * P, (k + 1) * P)
                        t = slice(half * HALF, (half + 1) * HALF)
                        mm = three(ps[:, g % 3, :], whi[u % 2][:, w], wlo[u % 2][:, w], uhi[:, k, t],
                                   ulo[:, k, t], k == 0, k == KT - 1)
                    if u == N_PROJ - 1 and half and part < 3:
                        mm.then_inc(s_ufree, 1)
                    if part == 3:
                        mm.then_inc(s_pmm, 1)
                elif kind == "O":
                    _, g, part = step
                    grp, m, half = g // 16, g % 16 // 2, g % 2
                    u = N_PROJ + g // 4 if grp < 2 else N_UNITS - 1
                    n_k = (4, 3, 1)[grp]
                    if part == 0:
                        if g < 3:
                            pe.wait_ge(s_pev, 2 * N_PROJ + g - 2)
                        elif g < 35:
                            pe.wait_ge(s_oadd, g - 2)
                        elif g == 35:
                            pe.wait_ge(s_st, NH * NC)
                        else:
                            pe.wait_ge(s_oadd, g - 3)
                        pe.wait_ge(s_wlo, u + 1)
                    for k in range(2 * part, min(2 * part + 2, n_k)):
                        if g % 16 == 0:
                            pe.wait_ge(s_mlo, (0, 4, 7)[grp] + k + 1)
                        w0 = m * P if grp == 2 else (m % 2 * n_k + k) * P
                        w, t = slice(w0, w0 + P), slice(half * HALF, (half + 1) * HALF)
                        mhi, mlo = ((mhi0[:, k, t], mlo0[:, k, t]) if grp == 0 else
                                    (mhi1[:, k, t], mlo1[:, k, t]) if grp == 1 else (mhi3[:, t], mlo3[:, t]))
                        mm = three(ps[:, out_bank(g), :], whi[u % 2][:, w], wlo[u % 2][:, w], mhi, mlo,
                                   k == 0, k == n_k - 1)
                    if k == n_k - 1:
                        mm.then_inc(s_omm, 1)
                elif kind == "AM":
                    i = step[1]
                    pe.wait_ge(s_asl, i + 1)
                    if i == 0:
                        pe.wait_ge(s_blk, 1)
                        pe.wait_ge(s_vev, 2 * NC)
                    else:
                        pe.wait_ge(s_aln, i)
                    for half in range(2):
                        t = slice(half * HALF, (half + 1) * HALF)
                        nc.tensor.matmul(ps[:, 3 + half, :], blkr[:, :], asqhi[:, t], start=True, stop=False)
                        nc.tensor.matmul(ps[:, 3 + half, :], blkr[:, :], asqlo[:, t], start=False, stop=True)\
                            .then_inc(s_ass, 1)
                elif kind == "SC":
                    i = step[1]
                    n, g = i // 2, i % 2
                    if i == 0:
                        pe.wait_ge(s_kqlo, 5)
                    else:
                        pe.wait_ge(s_masked, i)
                    rows = slice(HD * g, HD * g + HD)
                    qs, ks = slice(n * P, (n + 1) * P), slice(max(n - 1, 0) * P, max(n + 1, 2) * P)
                    for j in range(GRP):
                        mm = three(ps[:, 3 + j // 2, (j % 2) * 2 * P:(j % 2 + 1) * 2 * P], kqhi[rows, 1 + j, qs],
                                   kqlo[1 + j][rows, qs], kqhi[rows, 0, ks], kqlo[0][rows, ks], True, True)
                    mm.then_inc(s_scm, 1)
                elif kind == "TR":
                    i = step[1]
                    pe.wait_ge(s_prob, i + 1)
                    for b in range(nk(i) // P):
                        cur = b == nk(i) // P - 1
                        if cur and i:
                            pe.wait_ge(s_pte1, i)
                        if not cur and i > 2:
                            pe.wait_ge(s_pte0, i - 2)
                        for j in range(GRP):
                            mm = nc.tensor.transpose(ps[:, 6 if cur else 5, j * P:(j + 1) * P],
                                                     sc[:, i % 3, j, b * P:(b + 1) * P], ident[:, :])
                        mm.then_inc(s_tr, 1)
                elif kind == "PV":
                    i = step[1]
                    n, g = i // 2, i % 2
                    if g == 0 and n:
                        pe.wait_ge(s_attev, n)
                    if n:
                        pe.wait_ge(s_pte0, i - 1)
                    pe.wait_ge(s_pte1, i + 1)
                    out = ps[HD * g:HD * g + HD, 7, :]
                    vc = slice(NH * P + HD * g, NH * P + HD * g + HD)
                    if n:
                        nc.tensor.matmul(out, v[:, n - 1, vc], pT[:, 0, :], start=True, stop=False)
                    nc.tensor.matmul(out, v[:, n, vc], pT[:, 1, :], start=(n == 0), stop=True).then_inc(s_pv, 1)
                elif kind == "KT":
                    hh = step[1]
                    pe.wait_ge(s_kd, hh + 1)
                    if hh:
                        pe.wait_ge(s_cp, 14 * hh)
                        pe.wait_ge(s_st, NC * hh)
                    for c in range(NC):
                        mm = nc.tensor.transpose(ps[:, 3 + c // 4, (c % 4) * P:(c % 4 + 1) * P],
                                                 DD[1][:, c * P:(c + 1) * P], ident[:, :])
                        if c % 4 == 3:
                            mm.then_inc(s_kt, 1)
                elif kind == "LM":
                    _, hh, lv = step
                    pe.wait_ge(s_lvm, 2 * (7 * hh + lv + 1))
                    lhs, rhs = (M[lv % 2], M[lv % 2]) if lv else (rec[:, hh, :], M[0])
                    if lv == 0:
                        pe.wait_ge(s_kte, 2 * hh + 2)
                    for c in range(NC):
                        done = 2 * (7 * hh + lv - 1) + c // 4 + 1
                        if c % 4 == 0 and lv:
                            pe.wait_ge(s_cp, done)
                        cs = slice(c * P, (c + 1) * P)
                        mm = nc.tensor.matmul(ps[:, 3 + c // 4, (c % 4) * P:(c % 4 + 1) * P], lhs[:, cs], rhs[:, cs],
                                              start=True, stop=True)
                        if c % 4 == 3:
                            mm.then_inc(s_lmm, 1)
                elif kind == "OC":
                    _, hh, c = step
                    if c == 0:
                        pe.wait_ge(s_cp, 14 * (hh + 1))
                        pe.wait_ge(s_qi, hh + 1)
                        pe.wait_ge(*((s_oln, hh) if hh else (s_attev, NC)))
                    if c > 1:
                        pe.wait_ge(s_st, NC * hh + c - 1)
                    cs = slice(c * P, (c + 1) * P)
                    vh = v[:, c, hh * P:(hh + 1) * P]
                    out = ps[:, 5 + c // 4, (c % 4) * P:(c % 4 + 1) * P]
                    nc.tensor.matmul(ps[:, (7, 4)[c % 2], 0:P], KDT[:, c, :], vh, start=True, stop=True)\
                        .then_inc(s_kv, 1)
                    mm = nc.tensor.matmul(out, vh, A[:, cs], start=True, stop=(c == 0))
                    if c:
                        pe.wait_ge(s_st, NC * hh + c)
                        mm = nc.tensor.matmul(out, S[:, c % 2, :], qi(hh)[:, cs], start=False, stop=True)
                    mm.then_inc(s_oc, 1)
                elif kind == "OM":
                    hh = step[1]
                    pe.wait_ge(s_osq, hh + 1)
                    for half in range(2):
                        nc.tensor.matmul(ps[:, 5 + half, :], ones[:, :],
                                         on_tmp(hh)[:, half * HALF:(half + 1) * HALF],
                                         start=True, stop=True).then_inc(s_oss, 1)
                elif kind == "N2":
                    m = step[1]
                    for p in range(2):
                        if m == 0:
                            pe.wait_ge(s_flo, p + 1)
                        for half in range(2):
                            pe.wait_ge(s_u2lo, m + 2 if m else half + 1)
                            w, t = slice(m * P, (m + 1) * P), slice(half * HALF, (half + 1) * HALF)
                            mm = three(ps[:, ffn_bank(True, p, half), :], fhi[p][:, w], flo[p][:, w],
                                       u2hi[:, m, t], u2lo[:, m, t], m == 0, m == KT - 1)
                            if m == KT - 1:
                                mm.then_inc(s_fmm, 1)

            def ffn(i, first):
                for p in range(2 if first else 0, 4):
                    pe.wait_ge(s_flo, 6 * i + (p + 1))
                    for half in range(2):
                        t = slice(half * HALF, (half + 1) * HALF)
                        if first:
                            pe.wait_ge(*((s_oadd, 48) if p == 2 else (s_nln, half + 1)))
                        else:
                            pe.wait_ge(s_dadd, 16 * i + (2 * p + half) % 4 - 3)
                        for k in range(KT):
                            w = slice(k * P, (k + 1) * P)
                            mm = three(ps[:, ffn_bank(first, p, half), :], fhi[p][:, w], flo[p][:, w], u2hi[:, k, t],
                                       u2lo[:, k, t], k == 0, k == KT - 1)
                        mm.then_inc(s_fmm, 1)
                        if first and p == 2 and half == 0:
                            pe.wait_ge(s_nacc, KT - 1)
                            for x2 in range(2):
                                nc.tensor.matmul(ps[:, (2, 7)[x2], :], ones[:, :], nacc[:, x2 * HALF:(x2 + 1) * HALF],
                                                 start=True, stop=True).then_inc(s_nss, 1)
                for q in range(4):
                    for j in range(2):
                        if q == 0:
                            pe.wait_ge(s_flo, 6 * i + (4 + j + 1))
                            pe.wait_ge(s_hlo, 4 * i + (2 * j + 2))
                        for b in range(4):
                            m, half = 2 * q + b // 2, b % 2
                            if j == 0 and q > 1:
                                pe.wait_ge(s_dadd, 16 * i + (4 * (q - 2) + b + 1))
                            if j == 0 and q == 1 and b == 0:
                                pe.wait_ge(s_hid, 4 * i + 4)
                            w = slice(m * P, (m + 1) * P)
                            t = slice(half * HALF, (half + 1) * HALF)
                            mm = three(ps[:, down_bank(first, 4 * q + b), :], fhi[4 + j][:, w], flo[4 + j][:, w],
                                       hidhi[:, j, t], hidlo[:, j, t], j == 0, j == 1)
                            if j:
                                mm.then_inc(s_dmm, 1)

            ffn(0, True)
            with pe.Fori(1, FT // 2) as i:
                ffn(i, False)

        @block.vector
        def _(dve):
            def ffn_weights_lo(p, n):
                dve.wait_ge(s_fhi, n)
                nc.vector.tensor_tensor(flo[p][:, :], fraw[p][:, :], fhi[p][:, :].bitcast(F32), ALU.subtract)\
                    .then_inc(s_flo, 1)

            def value_weights_lo(n, i):
                c = slice(i * VW, (i + 1) * VW)
                dve.wait_ge(s_vhi, KT * n + i + 1)
                nc.vector.tensor_tensor(vlo[n][:, c], vraw[:, c], vhi[n][:, c].bitcast(F32), ALU.subtract)\
                    .then_inc(s_vlo, 1)

            for k in range(KT):
                value_weights_lo(0, k)
                dve.wait_ge(s_uhi, k + 1)
                nc.vector.scalar_tensor_tensor(ulo[:, k, :], x[:, k, :], g1[:, k:k + 1], uhi[:, k, :].bitcast(F32),
                                               ALU.mult, ALU.subtract).then_inc(s_ulo, 1)
            dve.wait_ge(s_const, 16 * N_CONST)
            nc.vector.tensor_tensor(lb_m, lb_in[:, 0:4], lb_in[:, 4:8], ALU.max).then_inc(s_lb, 1)
            dve.wait_ge(s_lb, 1)
            nc.vector.tensor_tensor(lb_e.rearrange("p (r h) -> p r h", r=2), lb_in.rearrange("p (r h) -> p r h", r=2),
                                    lb_m.unsqueeze(1).broadcast_to([P, 2, 4]), ALU.subtract).then_inc(s_lb, 1)
            nc.vector.tensor_scalar(nsink, sink, -1.0, None, ALU.mult)
            nc.vector.tensor_scalar(qg, qg, HD ** -0.5, None, ALU.mult)
            for i in range(KT):
                value_weights_lo(1, i)
            for step in order:
                kind = step[0]
                if kind == "WL":
                    u = step[1]
                    dve.wait_ge(s_whi, u + 1)
                    n = 6 * P if N_PROJ + 4 <= u < N_PROJ + 8 else 8 * P
                    nc.vector.tensor_tensor(wlo[u % 2][:, 0:n], wraw[u % 2][:, 0:n], whi[u % 2][:, 0:n].bitcast(F32),
                                            ALU.subtract).then_inc(s_wlo, 1)
                    if u == 1:
                        dve.wait_ge(s_lbact, 1)
                        nc.vector.tensor_tensor(lb_s, lb_e[:, 0:4], lb_e[:, 4:8], ALU.add).then_inc(s_lb, 1)
                        dve.wait_ge(s_lb, 3)
                        nc.vector.reciprocal(lb_s, lb_s).then_inc(s_lb, 1)
                        dve.wait_ge(s_lb, 4)
                        nc.vector.tensor_tensor(lb, lb_e[:, 0:4], lb_s, ALU.mult).then_inc(s_lb, 1)
                        nc.vector.tensor_tensor(omlb, lb_e[:, 4:8], lb_s, ALU.mult).then_inc(s_lb, 1)
                        dve.wait_ge(s_lb, 6)
                        nc.vector.tensor_scalar(nomlb, omlb, -1.0, None, ALU.mult).then_inc(s_lb, 1)
                        nc.vector.tensor_scalar(lb, lb, TINY, None, ALU.max).then_inc(s_lb, 1)
                elif kind == "P" and step[2] == 3:
                    g = step[1]
                    u, half = g // 2, g % 2
                    cols = slice(half * HALF, (half + 1) * HALF)
                    dve.wait_ge(s_pmm, g + 1)
                    if g == 0:
                        dve.wait_ge(s_rs, 1)
                    if u < 5:
                        dst = kq[:, u, cols]
                    else:
                        hh, j = divmod(u - 5, 3)
                        dst = (rawf, rawq, rawg[hh % 2])[j][:, cols]
                        if j == 0 and hh:
                            dve.wait_ge(s_lnf, hh)
                        if j < 2 and hh:
                            dve.wait_ge(s_kq, 2 * hh - 1 + j)
                        if j == 2 and hh >= 2:
                            dve.wait_ge(s_on, hh - 1)
                    nc.vector.tensor_tensor(dst, ps[:, g % 3, :], rs[:, cols], ALU.mult).then_inc(s_pev, 1)
                elif kind == "O" and step[2] == (1, 1, 0)[step[1] // 16]:
                    g = step[1]
                    m, half = g % 16 // 2, g % 2
                    dve.wait_ge(s_omm, g + 1)
                    if g < 16:
                        dve.wait_ge(s_x[m], 32)
                    else:
                        dve.wait_ge(s_oadd, g - 15)
                    hv = h[:, m, half * HALF:(half + 1) * HALF]
                    nc.vector.tensor_tensor(hv, ps[:, out_bank(g), :], hv, ALU.add).then_inc(s_oadd, 1)
                elif kind == "AN":
                    i = step[1]
                    dve.wait_ge(s_ars, i + 1)
                    nc.vector.scalar_tensor_tensor(kqn[i][:, :], kq[:, i, :], qg if i else kg, ars[:, :],
                                                   ALU.mult, ALU.mult).then_inc(s_an, 1)
                elif kind == "AD":
                    i = step[1]
                    dve.wait_ge(s_asq, i + 1)
                    dve.wait_ge(s_ash, i + 1)
                    nc.vector.tensor_tensor(asqlo[:, :], asq[:, i % 2, :], asqhi[:, :].bitcast(F32), ALU.subtract)\
                        .then_inc(s_asl, 1)
                elif kind == "AL":
                    i = step[1]
                    dve.wait_ge(s_kqhi, i + 1)
                    nc.vector.tensor_tensor(kqlo[i][:, :], kqn[i][:, :], kqhi[:, i, :].bitcast(F32),
                                            ALU.subtract).then_inc(s_kqlo, 1)
                elif kind == "SC":
                    i = step[1]
                    r, g, n_keys = i % 3, i % 2, nk(i)
                    dve.wait_ge(s_scm, i + 1)
                    if i == 0:
                        dve.wait_ge(s_setup, 1)
                    if i >= 3:
                        dve.wait_ge(s_tr, tr_count(i - 3))
                    sv = sc[:, r, :, 0:n_keys]
                    pv = ps[:, 3:5, :].rearrange("p b (j n) -> p (b j) n", j=2)[:, :, 0:n_keys]
                    mv = wmask[:, 2 * P - n_keys:2 * P].unsqueeze(1).broadcast_to([P, GRP, n_keys])
                    nc.vector.tensor_tensor(sv, pv, mv, ALU.add).then_inc(s_masked, 1)
                    dve.wait_ge(s_masked, i + 1)
                    nm = nmax[:, 4 * r:4 * r + 4]
                    nc.vector.tensor_reduce(nm, sv, AX.X, ALU.max, negate=True).then_inc(s_amx, 1)
                    dve.wait_ge(s_amx, i + 1)
                    nc.vector.tensor_tensor(nm, nm, nsink[:, GRP * g:GRP * g + GRP], ALU.min).then_inc(s_anm, 1)
                    dve.wait_ge(s_anm, i + 1)
                    nc.vector.tensor_tensor(esink[:, 4 * r:4 * r + 4], nm, sink[:, GRP * g:GRP * g + GRP], ALU.add)\
                        .then_inc(s_asn, 1)
                elif kind == "SN":
                    i = step[1]
                    q4 = slice(4 * (i % 3), 4 * (i % 3) + 4)
                    dve.wait_ge(s_exp, 5 * (i + 1))
                    nc.vector.tensor_tensor(den[:, q4], rsum[:, q4], esink[:, q4], ALU.add).then_inc(s_den, 1)
                    dve.wait_ge(s_den, i + 1)
                    nc.vector.reciprocal(rden[:, q4], den[:, q4]).then_inc(s_rden, 1)
                    dve.wait_ge(s_rden, i + 1)
                elif kind == "TR":
                    i = step[1]
                    dve.wait_ge(s_tr, tr_count(i))
                    if i:
                        dve.wait_ge(s_pv, i)
                    nc.vector.tensor_copy(pT[:, 1, :], ps[:, 6, :]).then_inc(s_pte1, 1)
                elif kind == "HK":
                    hh = step[1]
                    dve.wait_ge(s_sig, 3 * hh + 1)
                    if hh:
                        dve.wait_ge(s_lvm, 14 * hh)
                    nc.vector.tensor_scalar(K[:, :], rawf[:, :], nomlb[:, hh:hh + 1], omlb[:, hh:hh + 1],
                                            ALU.mult, ALU.add).then_inc(s_kq, 1)
                elif kind == "HQ":
                    hh = step[1]
                    dve.wait_ge(s_sig, 3 * hh + 2)
                    nc.vector.scalar_tensor_tensor(Q[:, :], rawq[:, :], P ** -0.5, DD[1][:, :], ALU.mult, ALU.mult)\
                        .then_inc(s_kq, 1)
                elif kind == "HS":
                    hh = step[1]
                    dve.wait_ge(s_lnf, hh + 1)
                    nc.vector.tensor_tensor_scan(B[:, :], scan_keep[:, :], B[:, :], 0.0, ALU.mult, ALU.add)\
                        .then_inc(s_scan, 1)
                elif kind == "H2":
                    hh = step[1]
                    dve.wait_ge(s_scan, hh + 1)
                    dve.wait_ge(s_kq, 2 * hh + 2)
                    bc = B[:, :].rearrange("p (c t) -> p c t", t=P)
                    dv = DD[1][:, :].rearrange("p (c t) -> p c t", t=P)
                    nc.vector.tensor_tensor(dv, bc[:, :, P - 1:P].broadcast_to([P, NC, P]), bc, ALU.subtract)\
                        .then_inc(s_d2, 1)
                elif kind == "HD":
                    hh = step[1]
                    dve.wait_ge(s_e2, hh + 1)
                    nc.vector.tensor_tensor(DD[1][:, :], K[:, :], DD[1][:, :], ALU.mult).then_inc(s_kd, 1)
                elif kind == "LX":
                    _, hh, lv = step
                    L = 1 << lv
                    dve.wait_ge(s_lve, 2 * (7 * hh + lv + 1))
                    if lv == 0:
                        if hh:
                            dve.wait_ge(s_lmm, 14 * hh)
                        nc.vector.tensor_tensor(M[0][:, :], Q[:, :], DD[0][:, :], ALU.mult).then_inc(s_lvm, 1)
                        if hh:
                            dve.wait_ge(s_oc, NC * hh)
                        nc.vector.tensor_tensor(rec[:, hh, :], K[:, :], M[1][:, :], ALU.mult).then_inc(s_lvm, 1)
                        continue
                    if lv == 1:
                        dve.wait_ge(s_lvm, 14 * hh + 2)
                    else:
                        dve.wait_ge(s_lmm, 2 * (7 * hh + lv - 1))
                    for up, src in ((0, K), (1, Q)):
                        mv, sv, ev = (a[:, :].rearrange("p (b u l) -> p b u l", u=2, l=L)[:, :, up, :]
                                      for a in (M[lv % 2], src, DD[lv % 2]))
                        nc.vector.tensor_tensor(mv, sv, ev, ALU.mult).then_inc(s_lvm, 1)
                elif kind == "LM":
                    _, hh, lv = step
                    for x2 in range(2):
                        dve.wait_ge(s_lmm, 2 * (7 * hh + lv) + x2 + 1)
                        if lv == 0 and x2 == 0:
                            dve.wait_ge(*((s_oc, NC * hh) if hh else (s_setup, 2)))
                        if lv:
                            dve.wait_ge(s_cp, 2 * (7 * hh + lv - 1) + x2 + 1)
                        av = A[:, x2 * HALF:(x2 + 1) * HALF].rearrange("p (c t) -> p c t", t=P)
                        nc.vector.copy_predicated(av, lmask[:, lv, :].unsqueeze(1).broadcast_to([P, 4, P]),
                                                  ps[:, 3 + x2, :].rearrange("p (c t) -> p c t", t=P))\
                            .then_inc(s_cp, 1)
                elif kind == "OC":
                    _, hh, c = step
                    dve.wait_ge(s_kv, NC * hh + c + 1)
                    st = ps[:, (7, 4)[c % 2], 0:P]
                    if c:
                        dve.wait_ge(s_st, NC * hh + c)
                        nc.vector.scalar_tensor_tensor(S[:, (c + 1) % 2, :], S[:, c % 2, :], ebt[:, 8 * (hh % 2) + c:8 * (hh % 2) + c + 1], st,
                                                       ALU.mult, ALU.add).then_inc(s_st, 1)
                    else:
                        dve.wait_ge(s_eb, 2 * hh + 2)
                        nc.vector.tensor_copy(S[:, 1, :], st).then_inc(s_st, 1)
                elif kind == "OX":
                    _, hh, part = step
                    if part == 0:
                        dve.wait_ge(s_ors, hh + 1)
                        nc.vector.scalar_tensor_tensor(rec[:, hh, :], rec[:, hh, :], og, on_tmp(hh)[:, :],
                                                       ALU.mult, ALU.mult).then_inc(s_on1, 1)
                    else:
                        dve.wait_ge(s_on1, hh + 1)
                        dve.wait_ge(s_gm, hh + 1)
                        nc.vector.tensor_tensor(rec[:, hh, :], rec[:, hh, :], rawg[hh % 2][:, :], ALU.mult)\
                            .then_inc(s_on, 1)
                elif kind == "ML":
                    i = step[1]
                    dve.wait_ge(s_mhi, i + 1)
                    if i < 4:
                        dst, src, hi = mlo0[:, i, :], att[:, i, :], mhi0[:, i, :]
                    elif i < 7:
                        dst, src, hi = mlo1[:, i - 4, :], rec[:, i - 4, :], mhi1[:, i - 4, :]
                    else:
                        dst, src, hi = mlo3[:, :], rec[:, 3, :], mhi3[:, :]
                    nc.vector.tensor_tensor(dst, src, hi.bitcast(F32), ALU.subtract).then_inc(s_mlo, 1)
                elif kind == "NL":
                    m = step[1]
                    for x2, cols in first_in_halves(m):
                        dve.wait_ge(s_u2hi, m + x2)
                        nc.vector.scalar_tensor_tensor(u2lo[:, m, cols], h[:, m, cols], g2[:, m:m + 1],
                                                       u2hi[:, m, cols].bitcast(F32), ALU.mult, ALU.subtract)\
                            .then_inc(s_u2lo, 1)
                elif kind == "F":
                    ffn_weights_lo(step[1], step[1] + 1)
            def ffn(i, first, last):
                for j in range(2):
                    for half in range(2):
                        dve.wait_ge(s_fmm, 8 * i + (4 * j + half + 1))
                        if first and not j and not half:
                            dve.wait_ge(s_nrs, 1)
                        nc.vector.tensor_tensor(gate[j][:, half, :], ps[:, ffn_bank(first, 2 * j, half), :],
                                                nrs[:, half * HALF:(half + 1) * HALF], ALU.mult).then_inc(s_gsc, 1)
                    for half in range(2):
                        r = 2 * j + half
                        dve.wait_ge(s_fmm, 8 * i + (4 * j + 2 + half + 1))
                        dve.wait_ge(s_gr, 4 * i + (r + 1))
                        nc.vector.tensor_tensor(hid[:, half, :], ps[:, ffn_bank(first, 2 * j + 1, half), :],
                                                gate[j][:, half, :], ALU.mult).then_inc(s_hid, 1)
                    for half in range(2):
                        r = 2 * j + half
                        dve.wait_ge(s_hhi, 4 * i + (r + 1))
                        t = slice(half * HALF, (half + 1) * HALF)
                        nc.vector.tensor_tensor(hidlo[:, j, t], hid[:, half, :], hidhi[:, j, t].bitcast(F32),
                                                ALU.subtract).then_inc(s_hlo, 1)
                    for p in () if last else (2 * j, 2 * j + 1):
                        ffn_weights_lo(p, 6 * i + (6 + p + 1))
                for g in range(16):
                    m, half = g // 2, g % 2
                    dve.wait_ge(s_dmm, 16 * i + (g + 1))
                    if not first:
                        dve.wait_ge(s_dadd, 16 * i + (-16 + g + 1))
                    hv = h[:, m, half * HALF:(half + 1) * HALF]
                    nc.vector.tensor_tensor(hv, ps[:, down_bank(first, g), :], hv, ALU.add)\
                        .then_inc(s_dadd, 1)
                for p in () if last else (4, 5):
                    ffn_weights_lo(p, 6 * i + (6 + p + 1))

            ffn(0, True, False)
            with dve.Fori(1, FT // 2 - 1) as i:
                ffn(i, False, False)
            ffn(FT // 2 - 1, False, True)


def kernel(x, norm1_gain, w_in, hgrn_lb_logits, hgrn_out_gain, q_norm_gain, k_norm_gain, attn_sinks, w_out,
           norm2_gain, w_ffn_gate, w_ffn_up, w_ffn_down):
    import numpy as np
    import concourse.bacc as bacc
    from concourse.bass_utils import run_bass_kernel_spmd

    def tiles(w):
        k, n = w.shape
        return w.reshape(k // P, P, n // P, P).transpose(2, 1, 0, 3).reshape(n // P, P, k)

    w = np.asarray(w_in)[0]
    hw = NH * P
    hq, hf, hi, hg = (w[:, i * hw:(i + 1) * hw] for i in range(4))
    aq = w[:, 4 * hw:4 * hw + AH * HD]
    ak, av = (w[:, 4 * hw + AH * HD + i * P:4 * hw + AH * HD + (i + 1) * P] for i in range(2))
    q_tiles = [np.concatenate([aq[:, i * HD:(i + 1) * HD], aq[:, (i + GRP) * HD:(i + GRP + 1) * HD]], 1)
               for i in range(GRP)]
    cols = [ak] + q_tiles
    for i in range(NH):
        cols += [a[:, i * P:(i + 1) * P] for a in (hf, hq, hg)]
    wproj = tiles(np.concatenate(cols, 1))
    wv = np.concatenate([hi, av], 1).reshape(KT, P, 2, VW).transpose(2, 1, 0, 3).reshape(2, P, KT * VW)
    wo = np.asarray(w_out)[0]
    ao = wo[hw:]
    att_rows = [np.concatenate([ao[i * HD:(i + 1) * HD], ao[(i + GRP) * HD:(i + GRP + 1) * HD]], 0)
                for i in range(GRP)]

    def pairs(rows):
        k = rows.shape[0]
        return tiles(rows).reshape(4, 2, P, k).transpose(0, 2, 1, 3).reshape(4, P, 2 * k)

    qg, kg = (np.concatenate([np.asarray(a)[0], np.asarray(a)[0]]).reshape(P, 1) for a in (q_norm_gain, k_norm_gain))
    arrays = {
        "xT": np.asarray(x)[0].T,
        "wv": wv,
        "wproj": wproj,
        "wo_a": pairs(np.concatenate(att_rows, 0)),
        "wo_b": pairs(wo[:3 * P]),
        "wo_c": wo[3 * P:hw],
        "wg": tiles(np.asarray(w_ffn_gate)[0]),
        "wu": tiles(np.asarray(w_ffn_up)[0]),
        "wd": np.asarray(w_ffn_down)[0].reshape(FT, P, D),
        "gain1": np.asarray(norm1_gain)[0].reshape(KT, P).T,
        "gain2": np.asarray(norm2_gain)[0].reshape(KT, P).T,
        "lbl": np.asarray(hgrn_lb_logits).reshape(2, NH, P).transpose(2, 0, 1).reshape(P, 2 * NH),
        "ogain": np.asarray(hgrn_out_gain)[0].reshape(P, 1),
        "qgain": qg,
        "kgain": kg,
        "sinks": np.broadcast_to(np.asarray(attn_sinks)[0], (P, AH)),
    }
    arrays = {n: np.ascontiguousarray(a) for n, a in arrays.items()}
    nc = bacc.Bacc("TRN2", target_bir_lowering=False, num_devices=1)
    args = [nc.dram_tensor(n, a.shape, mybir.dt.from_np(a.dtype), kind="ExternalInput").ap()
            for n, a in arrays.items()]
    y = nc.dram_tensor("yT", (D, T), F32, kind="ExternalOutput").ap()
    build(nc, *args, y)
    r = run_bass_kernel_spmd(nc, [arrays], core_ids=[0])
    return r.results[0]["yT"].T.reshape(1, T, D)
```
